# Optimizing a Trainium2 kernel written in Bass

```python
import jax, jax.numpy as jnp
from jax import lax
import numpy as np

D_MODEL = 1024
BATCH = 1
SEQ = 1024
DEPTH = 2
DEC_BATCH = 8
DEC_SEQ = 8
PAST_LEN = 4096
PAGE_SIZE = 128

N_MIXERS = 2
N_A_LAYERS = (DEPTH + 1) // 2
N_B_LAYERS = DEPTH // 2
CHUNK = 128
SGU_WIDTH = 2 * D_MODEL
SGU_GROUPS = 8
SGU_GROUP_DIM = SGU_WIDTH // SGU_GROUPS
HEAD_DIM = 64
N_HEADS = D_MODEL // HEAD_DIM
N_KV_HEADS = 4
GQA_GROUP = N_HEADS // N_KV_HEADS
WINDOW = 128
ROPE_THETA = 10000.0
D_FF = 2816
CONV_W = 3
EPS = 1e-6

kernel_name = 'hybrid_sgu_swa_convffn_step'

def rms_norm(x, g):
    xf = x.astype(jnp.float32)
    y = xf * lax.rsqrt(jnp.mean(xf * xf, axis=-1, keepdims=True) + EPS)
    return (y * g.astype(jnp.float32)).astype(x.dtype)

def layer_norm(x, g, b):
    xf = x.astype(jnp.float32)
    mu = jnp.mean(xf, axis=-1, keepdims=True)
    var = jnp.mean(jnp.square(xf - mu), axis=-1, keepdims=True)
    y = (xf - mu) * lax.rsqrt(var + EPS)
    return (y * g.astype(jnp.float32) + b.astype(jnp.float32)).astype(x.dtype)

def rope(x, pos):
    inv_freq = jnp.power(jnp.float32(ROPE_THETA), -jnp.arange(0, HEAD_DIM, 2, dtype=jnp.float32) / HEAD_DIM)
    ang = pos.astype(jnp.float32)[:, None] * inv_freq[None, :]
    cos = jnp.cos(ang)[None, :, None, :]
    sin = jnp.sin(ang)[None, :, None, :]
    xf = x.astype(jnp.float32)
    x1, x2 = jnp.split(xf, 2, axis=-1)
    return jnp.concatenate([x1 * cos - x2 * sin, x2 * cos + x1 * sin], axis=-1).astype(x.dtype)

def sgu_mixer(h, w_in, ln_g, ln_b, w_s, b_s, w_out):
    bsz, length, _ = h.shape
    z = jax.nn.gelu(h @ w_in)
    u, v = jnp.split(z, 2, axis=-1)
    v = layer_norm(v, ln_g, ln_b)
    n_chunks = -(-length // CHUNK)
    pad = n_chunks * CHUNK - length
    vp = jnp.pad(v, ((0, 0), (0, pad), (0, 0))).reshape(bsz, n_chunks, CHUNK, SGU_GROUPS, SGU_GROUP_DIM)
    causal = jnp.tril(jnp.ones((CHUNK, CHUNK), dtype=bool))
    w = jnp.where(causal[None], w_s, 0.0)
    mixed = jnp.einsum('gts,bnsgc->bntgc', w, vp) + b_s.T[:, :, None]
    mixed = mixed.reshape(bsz, n_chunks * CHUNK, SGU_WIDTH)[:, :length]
    return (u * mixed) @ w_out, v

def swa_project(h, w_qkv, q_norm, k_norm, pos):
    bsz, length, _ = h.shape
    qkv = h @ w_qkv
    q, k, v = jnp.split(qkv, [N_HEADS * HEAD_DIM, (N_HEADS + N_KV_HEADS) * HEAD_DIM], axis=-1)
    q = q.reshape(bsz, length, N_HEADS, HEAD_DIM)
    k = k.reshape(bsz, length, N_KV_HEADS, HEAD_DIM)
    v = v.reshape(bsz, length, N_KV_HEADS, HEAD_DIM)
    q = rope(rms_norm(q, q_norm), pos)
    k = rope(rms_norm(k, k_norm), pos)
    return q, k, v

def sink_attention(q, k, v, q_pos, k_pos, sinks):
    scale = HEAD_DIM ** -0.5
    logits = jnp.einsum('bnqkgd,bnskd->bnkgqs', q, k, preferred_element_type=jnp.float32) * scale
    rel = q_pos[:, :, None] - k_pos[:, None, :]
    valid = (rel >= 0) & (rel < WINDOW) & (k_pos[:, None, :] >= 0)
    logits = jnp.where(valid[None, :, None, None], logits, -jnp.inf)
    sink = sinks.astype(jnp.float32).reshape(1, 1, N_KV_HEADS, GQA_GROUP, 1, 1)
    m = jnp.maximum(jnp.max(logits, axis=-1, keepdims=True), sink)
    p = jnp.exp(logits - m)
    denom = jnp.sum(p, axis=-1, keepdims=True) + jnp.exp(sink - m)
    probs = (p / denom).astype(v.dtype)
    return jnp.einsum('bnkgqs,bnskd->bnqkgd', probs, v)

def swa_prompt(h, w_qkv, q_norm, k_norm, sinks, w_o):
    bsz, length, _ = h.shape
    pos = jnp.arange(length, dtype=jnp.int32)
    q, k, v = swa_project(h, w_qkv, q_norm, k_norm, pos)
    nb = length // WINDOW
    qb = q.reshape(bsz, nb, WINDOW, N_KV_HEADS, GQA_GROUP, HEAD_DIM)
    kb = k.reshape(bsz, nb, WINDOW, N_KV_HEADS, HEAD_DIM)
    vb = v.reshape(bsz, nb, WINDOW, N_KV_HEADS, HEAD_DIM)
    shift = ((0, 0), (1, 0), (0, 0), (0, 0), (0, 0))
    k_band = jnp.concatenate([jnp.pad(kb, shift)[:, :-1], kb], axis=2)
    v_band = jnp.concatenate([jnp.pad(vb, shift)[:, :-1], vb], axis=2)
    q_pos = pos.reshape(nb, WINDOW)
    k_pos = jnp.concatenate([q_pos - WINDOW, q_pos], axis=1)
    o = sink_attention(qb, k_band, v_band, q_pos, k_pos, sinks)
    y = o.reshape(bsz, length, N_HEADS * HEAD_DIM) @ w_o
    return y, k[:, -WINDOW:], v[:, -WINDOW:]

def swa_sample(h, buf_k, buf_v, w_qkv, q_norm, k_norm, sinks, w_o):
    bsz, length, _ = h.shape
    buf_len = buf_k.shape[1]
    pos = PAST_LEN + jnp.arange(length, dtype=jnp.int32)
    q, k, v = swa_project(h, w_qkv, q_norm, k_norm, pos)
    k_all = jnp.concatenate([buf_k, k], axis=1)
    v_all = jnp.concatenate([buf_v, v], axis=1)
    k_pos = jnp.concatenate([PAST_LEN - buf_len + jnp.arange(buf_len, dtype=jnp.int32), pos])
    qb = q.reshape(bsz, 1, length, N_KV_HEADS, GQA_GROUP, HEAD_DIM)
    o = sink_attention(qb, k_all[:, None], v_all[:, None], pos[None], k_pos[None], sinks)
    y = o.reshape(bsz, length, N_HEADS * HEAD_DIM) @ w_o
    return y, k_all[:, -WINDOW:], v_all[:, -WINDOW:]

def conv_ffn(h, past, norm_g, w_up, conv_w, conv_b, w_down):
    length = h.shape[1]
    a = rms_norm(h, norm_g) @ w_up
    a_ext = jnp.concatenate([past.astype(a.dtype), a], axis=1)
    c = conv_b + sum(conv_w[j] * a_ext[:, j:j + length] for j in range(CONV_W))
    gate, val = jnp.split(c, 2, axis=-1)
    y = (jax.nn.silu(gate) * val) @ w_down
    return y, a_ext[:, -(CONV_W - 1):]

def setup_inputs(seed: int = 0) -> dict:
    key = jax.random.key(seed)
    ks = jax.random.split(key, 32)
    f32 = jnp.float32
    nrm = lambda k, shape, scale: jax.random.normal(k, shape, f32) * scale
    qkv_out = (N_HEADS + 2 * N_KV_HEADS) * HEAD_DIM
    buf_len = min(WINDOW, PAST_LEN)
    return {
        'x_prompt': nrm(ks[0], (BATCH, SEQ, D_MODEL), 1.0),
        'x_sample': nrm(ks[1], (DEC_BATCH, DEC_SEQ, D_MODEL), 1.0),
        'cache_swa_k': nrm(ks[2], (N_B_LAYERS, DEC_BATCH, buf_len, N_KV_HEADS, HEAD_DIM), 1.0),
        'cache_swa_v': nrm(ks[3], (N_B_LAYERS, DEC_BATCH, buf_len, N_KV_HEADS, HEAD_DIM), 1.0),
        'state_ffn_conv': nrm(ks[4], (DEPTH, DEC_BATCH, CONV_W - 1, 2 * D_FF), 1.0),
        'mix_norm_g': 1.0 + nrm(ks[5], (DEPTH, D_MODEL), 0.02),
        'sgu_w_in': nrm(ks[6], (N_A_LAYERS, D_MODEL, 2 * SGU_WIDTH), D_MODEL ** -0.5),
        'sgu_ln_g': 1.0 + nrm(ks[7], (N_A_LAYERS, SGU_WIDTH), 0.02),
        'sgu_ln_b': nrm(ks[8], (N_A_LAYERS, SGU_WIDTH), 0.02),
        'sgu_w_s': nrm(ks[9], (N_A_LAYERS, SGU_GROUPS, CHUNK, CHUNK), CHUNK ** -0.5),
        'sgu_b_s': 1.0 + nrm(ks[10], (N_A_LAYERS, SGU_GROUPS, CHUNK), 0.1),
        'sgu_w_out': nrm(ks[11], (N_A_LAYERS, SGU_WIDTH, D_MODEL), SGU_WIDTH ** -0.5),
        'attn_w_qkv': nrm(ks[12], (N_B_LAYERS, D_MODEL, qkv_out), D_MODEL ** -0.5),
        'attn_q_norm': 1.0 + nrm(ks[13], (N_B_LAYERS, HEAD_DIM), 0.02),
        'attn_k_norm': 1.0 + nrm(ks[14], (N_B_LAYERS, HEAD_DIM), 0.02),
        'attn_sinks': nrm(ks[15], (N_B_LAYERS, N_HEADS), 1.0),
        'attn_w_o': nrm(ks[16], (N_B_LAYERS, N_HEADS * HEAD_DIM, D_MODEL), (N_HEADS * HEAD_DIM) ** -0.5),
        'ffn_norm_g': 1.0 + nrm(ks[17], (DEPTH, D_MODEL), 0.02),
        'ffn_w_up': nrm(ks[18], (DEPTH, D_MODEL, 2 * D_FF), D_MODEL ** -0.5),
        'ffn_conv_w': nrm(ks[19], (DEPTH, CONV_W, 2 * D_FF), CONV_W ** -0.5),
        'ffn_conv_b': nrm(ks[20], (DEPTH, 2 * D_FF), 0.02),
        'ffn_w_down': nrm(ks[21], (DEPTH, D_FF, D_MODEL), D_FF ** -0.5),
    }

def reference(x_prompt, x_sample, cache_swa_k, cache_swa_v, state_ffn_conv,
              mix_norm_g, sgu_w_in, sgu_ln_g, sgu_ln_b, sgu_w_s, sgu_b_s, sgu_w_out,
              attn_w_qkv, attn_q_norm, attn_k_norm, attn_sinks, attn_w_o,
              ffn_norm_g, ffn_w_up, ffn_conv_w, ffn_conv_b, ffn_w_down):
    yp, ys = x_prompt, x_sample
    sgu_v_s = []
    kp, vp, ksm, vsm = [], [], [], []
    conv_p, conv_s = [], []
    for layer in range(DEPTH):
        j = layer // N_MIXERS
        hp = rms_norm(yp, mix_norm_g[layer])
        hs = rms_norm(ys, mix_norm_g[layer])
        if layer % N_MIXERS == 0:
            sgu_args = (sgu_w_in[j], sgu_ln_g[j], sgu_ln_b[j], sgu_w_s[j], sgu_b_s[j], sgu_w_out[j])
            op, _ = sgu_mixer(hp, *sgu_args)
            os_, v_rows = sgu_mixer(hs, *sgu_args)
            sgu_v_s.append(v_rows)
        else:
            op, k_p, v_p = swa_prompt(hp, attn_w_qkv[j], attn_q_norm[j], attn_k_norm[j], attn_sinks[j], attn_w_o[j])
            os_, k_s, v_s = swa_sample(hs, cache_swa_k[j], cache_swa_v[j], attn_w_qkv[j], attn_q_norm[j],
                                       attn_k_norm[j], attn_sinks[j], attn_w_o[j])
            kp.append(k_p); vp.append(v_p); ksm.append(k_s); vsm.append(v_s)
        yp = yp + op
        ys = ys + os_
        zero_past = jnp.zeros((yp.shape[0], CONV_W - 1, 2 * D_FF), dtype=yp.dtype)
        fp, cp = conv_ffn(yp, zero_past, ffn_norm_g[layer], ffn_w_up[layer], ffn_conv_w[layer], ffn_conv_b[layer], ffn_w_down[layer])
        fs, cs = conv_ffn(ys, state_ffn_conv[layer], ffn_norm_g[layer], ffn_w_up[layer], ffn_conv_w[layer], ffn_conv_b[layer], ffn_w_down[layer])
        yp = yp + fp
        ys = ys + fs
        conv_p.append(cp); conv_s.append(cs)
    return (yp, ys, jnp.stack(sgu_v_s), jnp.stack(kp), jnp.stack(vp), jnp.stack(ksm), jnp.stack(vsm),
            jnp.stack(conv_p), jnp.stack(conv_s))


_drawn_inputs = setup_inputs


def setup_inputs(seed=0):
    import zlib

    import numpy as np

    out = dict(_drawn_inputs(seed))
    spreads = {}
    factors = {'sgu_ln_g': 2.84,
     'sgu_ln_b': 2.858,
     'attn_q_norm': 8.0,
     'attn_k_norm': 2.951,
     'attn_sinks': 61.281,
     'ffn_conv_b': 3.216}
    for name, (base, spread) in spreads.items():
        noise = np.random.default_rng([zlib.crc32(name.encode()), seed]).standard_normal(out[name].shape)
        drawn = base * np.exp(spread * noise) if base else spread * noise
        out[name] = __import__('jax').numpy.asarray(drawn.astype(out[name].dtype))
    for name, factor in factors.items():
        out[name] = (out[name] * factor).astype(out[name].dtype)
    return out
```

```python
import concourse.bass as bass
from concourse import mybir
from contextlib import ExitStack

import numpy as np

D = 1024
SEQ = 1024
NB, NT = 8, 8
SAMP = NB * NT
T = SEQ + SAMP
TT = 9
PAST_LEN = 4096
SGU = 2048
GROUPS = 8
DFF = 2816
FT = DFF // 128
FI = FT // 2
NH, NKV, HD = 16, 4, 64
QKV = (NH + 2 * NKV) * HD
EPS = 1e-6
KT = D // 128
CH = ((0, 384), (384, 384), (768, 320))
TOK0 = [128 * t for t in range(8)] + [T - 128]
AW = 2 + SEQ + NB * (2 + NT)
CW = AW - 2
STEP = 2 + NT
STAGE = 9

P_V = 0
P_U = P_V + 8
P_OUT = P_U + 8
P_F = [P_OUT + 8, 0]
P_QKV = P_F[0] + 3 * FI
P_WO = P_QKV + 6
P_F[1] = P_WO + 4
PAIRS = P_F[1] + 3 * FI if STAGE > 1 else P_QKV

A_U, B_U = 1, 1
A_O, B_O = A_U + 16, B_U + 16
A_F, B_F = [A_O + 4, 0], [B_O + 4, 0]
A_WO, B_WO = A_F[0] + 66, B_F[0] + 66
A_F[1], B_F[1] = A_WO + 4, B_WO + 4
A_END, B_END = (A_F[1] + 66, B_F[1] + 66) if STAGE > 1 else (A_WO, B_WO)

C_ID, C_CUR, C_CURT, C_PRVT, C_SEL, C_BLK, C_BLC, C_NEW, C_OLD, C_END = np.cumsum(
    [0, 128, 128, 128, 128, 128, 64, 128, 8, 128]).tolist()


def constants():
    c = np.zeros((128, C_END), np.float32)
    r = np.arange(128)
    c[:, C_ID:C_ID + 128] = r[:, None] == r[None, :]
    c[:, C_CUR:C_CUR + 128] = r[None, :] <= r[:, None]
    c[:, C_CURT:C_CURT + 128] = r[:, None] <= r[None, :]
    c[:, C_PRVT:C_PRVT + 128] = r[:, None] > r[None, :]
    q = np.arange(SAMP)
    c[:, C_SEL + 64:C_SEL + 128] = r[:, None] == (q % NT)[None, :]
    c[64:, C_BLK:C_BLK + 64] = (q // NT)[:, None] == (q // NT)[None, :]
    c[:64, C_BLC + 64:C_BLC + 128] = ((q // NT)[:, None] == (q // NT)[None, :]) & ((q % NT)[None, :] <= (q % NT)[:, None])
    c[:64, C_BLC:C_BLC + 64] = (q // NT)[:, None] == (q // NT)[None, :]
    c[:64, C_NEW:C_NEW + 8] = r[None, :8] <= (q % NT)[:, None]
    c[:64, C_OLD:C_OLD + 128] = r[None, :] > (q % NT)[:, None]
    inv = np.power(10000.0, -np.arange(0, HD, 2) / HD).astype(np.float32)
    pos = np.zeros((128, TT), np.float32)
    for t in range(TT):
        pos[:, t] = TOK0[t] + r
    pos[64:, 8] = PAST_LEN + q % NT
    ang = (pos[:, :, None] * inv[None, None, :]).astype(np.float32)
    ang = ang.astype(np.float64)
    rot = np.stack([np.cos(ang), np.sin(ang)], 1).astype(np.float32)
    return c, rot.reshape(128, 2 * TT * 32)


def step_program(nc, x_prompt, x_sample, cache_swa_k, cache_swa_v, state_ffn_conv, mix_norm_g, sgu_w_in, sgu_ln_g,
                 sgu_ln_b, sgu_w_s, sgu_b_s, sgu_w_out, attn_w_qkv, attn_q_norm, attn_k_norm, attn_sinks, attn_w_o,
                 ffn_norm_g, ffn_w_up, ffn_conv_w, ffn_conv_b, ffn_w_down, table, rotary,
                 y_prompt, y_sample, v_rows, k_prompt, v_prompt, k_sample, v_sample, conv_prompt, conv_sample):
    f32, f32r, i32 = mybir.dt.float32, mybir.dt.float32r, mybir.dt.int32
    ALU, ACT, AX = mybir.AluOpType, mybir.ActivationFunctionType, mybir.AxisListType
    mult, add, sub = ALU.mult, ALU.add, ALU.subtract

    with ExitStack() as ctx:
        ctx.enter_context(nc.allow_non_contiguous_dma(reason="small vectors"))

        def sb(name, shape, dt=f32, stack=ctx):
            return stack.enter_context(nc.sbuf_tensor(name, shape, dt))

        def sem(name):
            return ctx.enter_context(nc.semaphore(name))

        idn = sb("idn", [128, 128])
        ones = sb("ones", [128, 128])
        gains = sb("gains", [128, 32])
        cw = sb("cw", [128, 2, 2, 2, 2 * FT])
        eps = sb("eps", [128, 1])
        ss = sb("ss", [128, 16])
        rt = sb("rt", [128, 16])
        xm = sb("xm", [128, TT, 128])
        wraw = sb("wraw", [128, 2, 1024])
        wh = sb("wh", [128, 2, 1024], f32r)
        wl = sb("wl", [128, 2, 1024], f32r)
        with ExitStack() as s:
            x = sb("x", [128, KT, T], stack=s)
            hh = sb("hh", [128, KT, T], f32r, s)
            hl = sb("hl", [128, KT, T], f32r, s)
            v = sb("v", [128, 16, TT, 128], stack=s)
        with ExitStack() as s:
            tabs = sb("tabs", [128, C_END], stack=s)
            selr = sb("selr", [128, 128], f32r, s)
            sb("gap0", [128, 34816 // 4 - C_END - 128], stack=s)
            sb("gap1", [128, 2 * KT * T], stack=s)
            xin = sb("xin", [128, TT, D], stack=s)
            junk = sb("junk", [128, D], stack=s)
            vecs = sb("vecs", [128, 5, 128], stack=s)
            wsr = sb("wsr", [128, GROUPS, 128], stack=s)
        with ExitStack() as s:
            vnh = sb("vnh", [128, TT, 128], f32r, s)
            vnl = sb("vnl", [128, TT, 128], f32r, s)
            u = sb("u", [128, T], stack=s)
            wth = sb("wth", [128, GROUPS, 128], f32r, s)
            wtl = sb("wtl", [128, GROUPS, 128], f32r, s)
            wsh = sb("wsh", [128, GROUPS, 64], f32r, s)
            wsl = sb("wsl", [128, GROUPS, 64], f32r, s)
            bsb = sb("bsb", [128, GROUPS, 128], stack=s)
            lng = sb("lng", [128, 2, 128], stack=s)
            lnb = sb("lnb", [128, 2, 128], stack=s)
            bst = sb("bst", [128, TT, 8, 6], stack=s)
            mv = sb("mv", [128, TT, 2], stack=s)
        with ExitStack() as s:
            sb("gap2", [128, KT * T], stack=s)
            gh = sb("gh", [128, 16, T], f32r, s)
            with ExitStack() as s2:
                gt = sb("gt", [128, 16, T], stack=s2)
            with ExitStack() as s2:
                gl = sb("gl", [128, 16, T], f32r, s2)
                ssum = sb("ssum", [128, T], stack=s2)
                sqt = sb("sqt", [128, T // 2], stack=s2)
        with ExitStack() as s:
            sb("gap3", [128, 3 * KT * T], stack=s)
            fh = sb("fh", [128, 3, T], f32r, s)
            fl = sb("fl", [128, 3, T], f32r, s)
            a_sb = sb("a_sb", [128, 2, AW + 10], stack=s)
            cv = sb("cv", [128, AW], stack=s)
            with ExitStack() as s2:
                cg = sb("cg", [128, AW], stack=s2)
                sg = sb("sg", [128, AW], stack=s2)
            with ExitStack() as s2:
                fhx = sb("fhx", [128, 1, T], f32r, s2)
                sb("gap9", [128, AW - T], stack=s2)
                flx = sb("flx", [128, 1, T], f32r, s2)
            sb("gap10", [128, 2 * AW], stack=s)
            mt = sb("mt", [128, T], stack=s)
            rbc = sb("rbc", [128, T], stack=s)
            stc = sb("stc", [128, 4, 18], stack=s)
            sto = sb("sto", [18, 4, 128], stack=s)
            pst = sb("pst", [16, 4, 128], stack=s)
        with ExitStack() as s:
            sb("gap5", [128, KT * T], stack=s)
            with ExitStack() as s2:
                kT = sb("kT", [128, 2, NKV, 128], stack=s2)
                vb = sb("vb", [128, 2, NKV * HD], stack=s2)
                qTe = sb("qTe", [128, KT, 128], stack=s2)
                with ExitStack() as s3:
                    qr = sb("qr", [128, 20 * HD], stack=s3)
                    t1 = sb("t1", [128, 2, 20 * HD], stack=s3)
                    with ExitStack() as s4:
                        t0 = sb("t0", [128, 2, 20 * HD], stack=s4)
                    sm = sb("sm", [128, 2, 512], stack=s3)
                    pr = sb("pr", [128, 2, 512], stack=s3)
                    pc = sb("pc", [128, 2, 512], stack=s3)
                    pp = sb("pp", [128, 2, 512], stack=s3)
                    qTo = sb("qTo", [128, KT, 128], stack=s3)
                with ExitStack() as s3:
                    qm = sb("qm", [128, KT, NB * 72], stack=s3)
                    kcT = sb("kcT", [128, NB, NKV, 128], stack=s3)
                    ssc = sb("ssc", [64, 16, 128], stack=s3)
                    with ExitStack() as s4:
                        vc = sb("vc", [128, NB, NKV * HD], stack=s4)
                        kc = sb("kc", [128, NB, NKV * HD], stack=s4)
                    with ExitStack() as s4:
                        sb("gap7", [64, NB * NKV * HD], stack=s4)
                        pn = sb("pn", [64, 16, 128], stack=s4)
                with ExitStack() as s3:
                    pcT = sb("pcT", [128, 16, 64], stack=s3)
                    pnT = sb("pnT", [128, 16, 64], stack=s3)
            sb("gap6", [128, 2 * KT * T], stack=s)
            qkv = sb("qkv", [128, TT, QKV], stack=s)
            rot = sb("rot", [128, 2, TT, 32], stack=s)
            tb2 = sb("tb2", [128, C_END], stack=s)
            gqk = sb("gqk", [128, 2, HD], stack=s)
            nsk = sb("nsk", [128, NH], stack=s)
            pbias = sb("pbias", [128, 8], stack=s)
            hs = sb("hs", [128, TT, 20], stack=s)
            rq = sb("rq", [128, TT], stack=s)
            stt = sb("stt", [128, 64], stack=s)
            tmp = sb("tmp", [128, 1024], stack=s)
        with ExitStack() as s:
            sb("gap4", [128, KT * T], stack=s)
            yst = sb("yst", [128, 2, TT, 128], stack=s)

        ps = ctx.enter_context(nc.psum_tensor("ps", [128, 8, 512], f32))
        BANK = (0, 3)
        STATS = (1, 2, 3)

        w_in = [sem("w_in0"), sem("w_in1")]
        w_hi, w_lo = sem("w_hi"), sem("w_lo")
        w_used = sem("w_used")
        free = [sem("free_a"), sem("free_b")]
        t_in, x_in = sem("t_in"), [sem(f"x_in{i}") for i in range(5)]
        vec_in, ws_in, bs_in = sem("vec_in"), sem("ws_in"), sem("bs_in")
        sq_st, rt_sq, rt_rc, xn = sem("sq_st"), sem("rt_sq"), sem("rt_rc"), sem("xn")
        ws_msk, vec_t, vec_ok = sem("ws_msk"), sem("vec_t"), sem("vec_ok")
        ws_t, wt_hi, wt_lo, ws8_t, ws8_ok, sel_ok = (sem(n) for n in ("ws_t", "wt_hi", "wt_lo", "ws8_t", "ws8_ok", "sel_ok"))
        ones_ok, eps_ok = sem("ones_ok"), sem("eps_ok")
        x_t, h_hi, h_lo = sem("x_t"), sem("h_hi"), sem("h_lo")
        zero = sem("zero")
        tm_full, tm_free = sem("tm_full"), sem("tm_free")
        bn, bna, ln_sq, ln_rc = sem("bn"), sem("bna"), sem("ln_sq"), sem("ln_rc")
        ln_in = [sem("ln_in0"), sem("ln_in1")]
        ln, vn_hi, vn_lo, v_out = sem("ln"), sem("vn_hi"), sem("vn_lo"), [sem("v_out0"), sem("v_out1")]
        u_ok, mixed, mix_b, gated = sem("u_ok"), sem("mixed"), sem("mix_b"), sem("gated")
        g_hi, g_lo, xm_in, xm_used = sem("g_hi"), sem("g_lo"), sem("xm_in"), sem("xm_used")
        x_sq, x_ss, x_ok = sem("x_sq"), sem("x_ss"), sem("x_ok")
        stat, rb_sq, rb_ok = sem("stat"), sem("rb_sq"), sem("rb_ok")
        halo, conv0, conv, silu, mtok, f_hi, f_lo = (sem(n) for n in ("halo", "conv0", "conv", "silu", "mtok", "f_hi", "f_lo"))
        down = sem("down")
        past_in, past_t, state_c, state_t, state_o, state_out = (
            sem(n) for n in ("past_in", "past_t", "state_c", "state_t", "state_o", "state_out"))
        a_in, stats_q, rq_sq, rq_ok = sem("a_in"), sem("stats_q"), sem("rq_sq"), sem("rq_ok")
        q_sq, hs_ok, hs_sq, hs_rc, nsk_ok = sem("q_sq"), sem("hs_ok"), sem("hs_sq"), sem("hs_rc"), sem("nsk_ok")
        zero_a, nrm, rope0, rope, qk_t, qk_c, v_c = sem("zero_a"), sem("nrm"), sem("rope0"), sem("rope"), sem("qk_t"), sem("qk_c"), sem("v_c")
        s_full, s_cp, s_mrg, s_nm = sem("s_full"), sem("s_cp"), sem("s_mrg"), sem("s_nm")
        p_exp, p_nrm, p_t, p_msk = sem("p_exp"), sem("p_nrm"), sem("p_t"), sem("p_msk")
        o_full, o_ok = sem("o_full"), sem("o_ok")
        kc_in, kv_in, kv_out, kc_t, kc_c, smp = sem("kc_in"), sem("kv_in"), sem("kv_out"), sem("kc_t"), sem("kc_c"), sem("smp")
        z_q, z_s, z_n, z_a, z_t, z_tc = (sem(n) for n in ("z_q", "z_s", "z_n", "z_a", "z_t", "z_tc"))
        hold_act, hold_dve, hold_pool = sem("hold_act"), sem("hold_dve"), sem("hold_pool")
        y_t, y_c, y_out = sem("y_t"), sem("y_c"), [sem("y_out0"), sem("y_out1")]

        block = ctx.enter_context(nc.Block())

        def at(c, m=0, i=None):
            return c if i is None else i * m + c

        def load(eng, src, s, k, p, m=0, i=None):
            if i is not None or p > 0:
                eng.wait_ge(w_lo, at(2 * p + s - 1, 2 * m, i))
            eng.dma_start(wraw[:, s, :].rearrange("p (k n) -> p k n", k=k),
                          src.rearrange("(k p) n -> p k n", p=128)).then_inc(w_in[s], 16)

        def hi(act, s, p, m=0, i=None):
            act.wait_ge(w_in[s], at(16 * (p + 1), 16 * m, i))
            if i is not None or p > 0:
                act.wait_ge(w_used, at(2 * p + s - 1, 2 * m, i))
            act.activation(wh[:, s, :], wraw[:, s, :], ACT.Copy).then_inc(w_hi, 1)

        def lo(dve, s, p, m=0, i=None):
            dve.wait_ge(w_hi, at(2 * p + s + 1, 2 * m, i))
            dve.tensor_tensor(wl[:, s, :], wraw[:, s, :], wh[:, s, :].bitcast(f32), sub).then_inc(w_lo, 1)

        def chunks(area, width=None):
            b = BANK[area]
            return ps[:, b:b + 2, 0:384], ps[:, b + 2, 0:320]

        def cut(row):
            return row[:, 0:768].rearrange("p (c n) -> p c n", c=2), row[:, 768:T]

        def passes(s):
            return ((wh, 0), (wh, 1), (wl, 0))

        def rows(pe, area, s, k, col, mov, start, stop):
            for n, (w, part) in enumerate(passes(s)):
                for c, (c0, cn) in enumerate(CH):
                    ins = pe.matmul(ps[:, BANK[area] + c, 0:cn], w[:, s, col:col + 128], mov[part][:, k, c0:c0 + cn],
                                    start=start and n == 0, stop=stop and n == 2, skip_group_check=True)
            return ins

        def square_slot(n, h):
            return sqt[:, :] if n == 0 else xm[:, :, :].rearrange("p t n -> p (t n)")[:, h * (T // 2):(h + 1) * (T // 2)]

        x_mov, g_mov = (hh, hl), (gh, gl)

        S_BANK = ((3, 4), (5, 6))
        GROUPS_A = 4 * 8

        def piece_at(c):
            n, g = c // 4, c % 4
            return (n + 2, g - 2) if g >= 2 else (n + 1, 2) if g == 0 else None

        def for_steps(eng, step):
            for c in range(4):
                step(c)
            with eng.Fori(0, 3) as i:
                for c in range(4, 12):
                    step(c, i)
            for c in range(28, GROUPS_A):
                step(c)

        def attention_loads(sp):
            def qkv_pair(c, p, m=0, i=None):
                for s in range(2):
                    load(sp, attn_w_qkv[0, 512 * s:512 * s + 512, bass.ds(at(256 * c, 256 * m, i), 256)], s, 4, p, m, i)
            qkv_pair(0, P_QKV)
            sp.wait_ge(w_used, 2 * P_QKV)
            sp.wait_ge(state_out, 32 * FI)
            sp.dma_start(rot[:, :, :, :].rearrange("p a t n -> p (a t n)"), rotary).then_inc(a_in, 16)
            sp.dma_start(tb2[:, :], table).then_inc(a_in, 16)
            sp.dma_start(gqk[:, 0, :], attn_q_norm[0].partition_broadcast(128)).then_inc(a_in, 16)
            sp.dma_start(gqk[:, 1, :], attn_k_norm[0].partition_broadcast(128)).then_inc(a_in, 16)
            sp.dma_start(nsk[:, :], attn_sinks[0].partition_broadcast(128)).then_inc(a_in, 16)
            with sp.Fori(0, 5) as i:
                qkv_pair(1, P_QKV + 1, 1, i)

            def wo_pair(c, p, m=0, i=None):
                for s in range(2):
                    load(sp, attn_w_o[0, :, bass.ds(at(256 * c + 128 * s, 256 * m, i), 128)], s, 8, p, m, i)
            wo_pair(0, P_WO)
            for src, dst in ((cache_swa_k, k_sample), (cache_swa_v, v_sample)):
                sp.dma_start(dst[0, :, 0:128 - NT].rearrange("b w h d -> b (w h d)"),
                             src[0, :, NT:128].rearrange("b w h d -> b (w h d)")).then_inc(kv_out, 16)
            sp.wait_ge(rope, ROPE * 7)
            sp.dma_start(k_prompt[0, 0].rearrange("w h d -> w (h d)"), qr[:, 1024:1280]).then_inc(kv_out, 16)
            sp.dma_start(v_prompt[0, 0].rearrange("w h d -> w (h d)"), qkv[:, 7, 1280:1536]).then_inc(kv_out, 16)
            sp.wait_ge(w_used, 2 * P_WO)
            sp.dma_start(kc[:, :, :], cache_swa_k[0].rearrange("b w h d -> w b (h d)")).then_inc(kc_in, 16)
            sp.wait_ge(o_ok, GROUPS_A)
            sp.dma_start(vc[:, :, :], cache_swa_v[0].rearrange("b w h d -> w b (h d)")).then_inc(kv_in, 16)
            with sp.Fori(0, 3) as i:
                wo_pair(1, P_WO + 1, 1, i)

        def attention_pool(pool):
            pool.wait_ge(w_used, 2 * P_WO)
            pool.memset(kT[:, 1, :, :], 0.0).then_inc(zero_a, 1)
            pool.memset(vb[:, 1, :], 0.0).then_inc(zero_a, 1)
            pool.memset(pbias[:, :], 0.0).then_inc(zero_a, 1)
            pool.wait_ge(zero_a, 3)
            pool.memset(pbias[:, 0:1], -1e30).then_inc(zero_a, 1)
            rotate(pool, t1, rope, 1)
            with pool.Fori(0, 6) as i:
                rotate(pool, t1, rope, 2, i)
            rotate(pool, t1, rope, 8)
            pool.wait_ge(qk_t, 27)
            pool.wait_ge(smp, 2 * NB * 16)
            pool.wait_ge(o_ok, GROUPS_A)
            pool.memset(qm[:, :, :], 0.0).then_inc(zero_a, 1)
            pool.wait_ge(kc_t, NB)
            pool.memset(pn[:, :, :], 0.0).then_inc(zero_a, 1)

        ROPE = 6

        def attention_act(act, squares):
            def qkv_block(b, m=0, i=None, values=False):
                hi(act, 0, P_QKV + 1 + b, m, i)
                for t in range(0, TT, 2):
                    bank = t // 2
                    if t < 8:
                        act.wait_ge(tm_full, at(32 + 4 * b + bank + 1, 4 * m, i))
                    else:
                        act.wait_ge(w_used, at(2 * (P_QKV + b) + 2, 2 * m, i))
                    if values:
                        pass
                    elif i is not None:
                        n = 5 * b + (0 if bank == 0 else -1 if bank == 1 else bank - 1)
                        act.wait_ge(hs_ok, at(n, 5 * m, i))
                    elif bank >= 2:
                        act.wait_ge(hs_ok, bank - 1)
                    for t_ in range(t, min(t + 2, TT)):
                        src = ps[:, bank, 256 * (t_ - t):256 * (t_ - t) + 256]
                        ins = act.activation(qkv[:, t_, bass.ds(at(256 * b, 256 * m, i), 256)], src, ACT.Copy,
                                             scale=rq[:, t_:t_ + 1])
                        if not values:
                            ins = act.activation(tmp[:, 512 * (bank % 2) + 256 * (t_ - t):512 * (bank % 2) + 256 * (t_ - t) + 256],
                                             src, ACT.Square, scale=rq[:, t_:t_ + 1])
                    ins.then_inc(tm_free, 1)
                hi(act, 1, P_QKV + 1 + b, m, i)

            act.wait_ge(stat, 2)
            act.activation(rq[:, :], ps[:, 6, 0:TT], ACT.Sqrt, scale=1.0 / D, bias=eps[:, :]).then_inc(rq_sq, 1)
            act.wait_ge(rq_ok, 1)
            act.wait_ge(state_out, 32 * FI)
            qkv_block(0)
            with act.Fori(0, 4) as i:
                qkv_block(1, 1, i)
            act.wait_ge(hs_ok, 25)
            act.activation(hs[:, :, :], hs[:, :, :], ACT.Sqrt, scale=1.0 / HD, bias=eps[:, :]).then_inc(hs_sq, 1)
            qkv_block(5, values=True)

            def take_piece(n, j, i=None):
                act.wait_ge(qk_t, at(3 * n + j + 1, 6, i))
                dst = (qTe, qTo)[n % 2][:, 4 * j:4 * j + 4, :] if j < 2 else kT[:, n % 2, :, :]
                act.activation(dst.rearrange("p k n -> p (k n)"), ps[:, 0, :], ACT.Copy).then_inc(qk_c, 1)

            def take_v(n, i=None):
                if n:
                    act.wait_ge(o_full, at(4 * n, 8, i))
                if i is not None:
                    act.sem_inc(hold_act, 1)
                act.activation(vb[:, n % 2, :], qkv[:, bass.ds(at(n, 2, i), 1), 1280:1536].rearrange("p o n -> p (o n)"),
                               ACT.Copy).then_inc(v_c, 1)

            def copy_prev(c, i=None):
                act.wait_ge(s_full, at(c + 1, 8, i))
                if c >= 2:
                    act.wait_ge(p_exp, at(c - 1, 8, i))
                b = S_BANK[c % 2][0]
                first = 0 if c < 4 and i is None else 1
                act.activation(sm[:, c % 2, :].rearrange("p (e n) -> p e n", e=2), ps[:, b:b + 2, 256:512], ACT.Identity,
                               bias=pbias[:, first:first + 1]).then_inc(s_cp, 1)

            def exps(c, i=None):
                z = c % 2
                act.wait_ge(s_nm, at(2 * c + 2, 16, i))
                if c >= 2:
                    act.wait_ge(p_t, at(c - 1, 8, i))
                for h in range(4):
                    act.activation(pr[:, z, 128 * h:128 * h + 128], sm[:, z, 128 * h:128 * h + 128], ACT.Exp,
                                   bias=stt[:, 8 * z + h:8 * z + h + 1], scale=HD ** -0.5,
                                   accum_out=stt[:, 16 + 8 * z + h:17 + 8 * z + h])
                act.activation(stt[:, 20 + 8 * z:24 + 8 * z], stt[:, 4 + 8 * z:8 + 8 * z], ACT.Exp).then_inc(p_exp, 1)

            def take_o(c, i=None):
                g = c % 4
                act.wait_ge(o_full, at(c + 1, 8, i))
                if i is not None:
                    act.sem_inc(hold_act, 1)
                act.activation(qkv[:, bass.ds(at(c // 4, 2, i), 1), 256 * g:256 * g + 256].rearrange("p o n -> p (o n)"),
                               ps[:, 1 + c % 2, 0:256], ACT.Copy).then_inc(o_ok, 1)

            def step(c, i=None):
                more = i is not None or c + 3 < GROUPS_A
                if more:
                    copy_prev(c + 3, i)
                piece = piece_at(c)
                if piece is not None and piece[0] <= 8:
                    take_piece(*piece, i)
                if c % 4 == 3:
                    take_v(c // 4 + 1, i)
                take_o(c, i)
                if more:
                    exps(c + 3, i)

            act.wait_ge(zero_a, 4)
            for j in range(3):
                take_piece(0, j)
            take_v(0)
            copy_prev(0)
            copy_prev(1)
            exps(0)
            copy_prev(2)
            take_piece(1, 0)
            take_piece(1, 1)
            exps(1)
            exps(2)
            for_steps(act, step)

            act.wait_ge(rope, ROPE * 8)
            for b in range(NB):
                act.dma_start(k_sample[0, b, 128 - NT:128].rearrange("w h d -> w (h d)"),
                              qr[64 + NT * b:64 + NT * b + NT, 1024:1280]).then_inc(smp, 16)
                act.dma_start(v_sample[0, b, 128 - NT:128].rearrange("w h d -> w (h d)"),
                              qkv[64 + NT * b:64 + NT * b + NT, 8, 1280:1536]).then_inc(smp, 16)
            act.wait_ge(smp, 2 * NB * 16)
            act.wait_ge(rope, ROPE * 8)
            for b in range(0, NB):
                act.wait_ge(kc_t, b + 1)
                act.activation(kcT[:, b, :, :].rearrange("p g n -> p (g n)"), ps[:, 3 + b % 4, :], ACT.Copy).then_inc(kc_c, 1)
            act.wait_ge(z_s, 1)
            act.activation(ssc[:, :, :].rearrange("p (a h) n -> p a (h n)", a=4), ps[0:64, 3:7, :], ACT.Copy).then_inc(z_a, 1)
            act.wait_ge(z_n, 6)
            act.activation(ssc[:, :, :], ssc[:, :, :], ACT.Exp).then_inc(z_a, 1)
            act.activation(stt[0:64, 32:48], stt[0:64, 16:32], ACT.Exp).then_inc(z_a, 1)
            act.wait_ge(z_t, 1)
            act.activation(pcT[:, :, :].rearrange("p (a h) n -> p a (h n)", a=2), ps[:, 3:5, :], ACT.Copy).then_inc(z_tc, 1)
            act.wait_ge(z_t, 2)
            act.activation(pnT[:, :, :].rearrange("p (a h) n -> p a (h n)", a=2), ps[:, 5:7, :], ACT.Copy).then_inc(z_tc, 1)
            act.wait_ge(z_t, 3)
            act.activation(qkv[:, 8, 0:1024].rearrange("p (k n) -> p k n", k=KT)[:, :, 0:64],
                           ps[:, 2, :].rearrange("p (k n) -> p k n", k=KT), ACT.Copy).then_inc(o_ok, 1)

            act.wait_ge(o_ok, GROUPS_A + 1)
            for k in range(KT):
                act.activation(hh[:, k, 0:SEQ].rearrange("p (t n) -> p t n", n=128), qkv[:, 0:8, 128 * k:128 * k + 128], ACT.Copy)
                act.activation(hh[:, k, SEQ:T], qkv[:, 8, 128 * k:128 * k + 64], ACT.Copy).then_inc(h_hi, 1)
            for m in range(8):
                act.wait_ge(w_used, 2 * P_WO + m + 1)
                hi(act, m % 2, P_WO + 1 + m // 2)
                act.wait_ge(free[m % 2], (A_WO, B_WO)[m % 2] + m // 2 + 1)
                if m < 7:
                    squares(2, m)

        def rotate(eng, t, turned, n, i=None):
            ti = bass.ds(at(n, 1, i), 1)
            r0 = ROPE * max(n - 1, 0)

            def after(semaphore, k, m):
                eng.wait_ge(semaphore, at(k, m, i))
                if i is not None:
                    eng.sem_inc(hold_pool, 1)

            def halves(a):
                return a.rearrange("p (h c d) -> p h c d", c=2, d=32)

            if n >= 2:
                after(turned, r0, ROPE)
            after(nrm, 2 * n + 2, 2)
            src = halves(qkv[:, ti, 0:1280].rearrange("p o n -> p (o n)"))
            cos = rot[:, 0, ti, :].rearrange("p o n -> p (o n)").unsqueeze(1).to_broadcast([128, 20, 32])
            sin = rot[:, 1, ti, :].rearrange("p o n -> p (o n)").unsqueeze(1).to_broadcast([128, 20, 32])
            for c in range(2):
                eng.tensor_tensor(halves(t[:, 0, :])[:, :, c, :], src[:, :, c, :], cos, mult).then_inc(turned, 1)
                eng.tensor_tensor(halves(t[:, 1, :])[:, :, c, :], src[:, :, 1 - c, :], sin, mult).then_inc(turned, 1)
            after(turned, r0 + 4, ROPE)
            if n:
                after(qk_t, 3 * n, 3)
            if n == 8:
                eng.wait_ge(kv_out, 16 * 4)
            for c, op in ((0, sub), (1, add)):
                eng.tensor_tensor(halves(qr[:, :])[:, :, c, :], halves(t[:, 0, :])[:, :, c, :], halves(t[:, 1, :])[:, :, c, :],
                                  op).then_inc(turned, 1)

        def attention_dve(dve):
            dve.wait_ge(rq_sq, 1)
            dve.reciprocal(rq[:, :], rq[:, :]).then_inc(rq_ok, 1)
            dve.wait_ge(a_in, 80)
            dve.tensor_scalar(nsk[:, :], nsk[:, :], -1.0, None, mult).then_inc(nsk_ok, 1)

            def sums(b, m=0, i=None):
                lo(dve, 0, P_QKV + 1 + b, m, i)
                for t in range(0, TT, 2):
                    bank, tn = t // 2, min(2, TT - t)
                    dve.wait_ge(tm_free, at(40 + 5 * b + bank + 1, 5 * m, i))
                    dve.tensor_reduce(hs[:, t:t + tn, bass.ds(at(4 * b, 4 * m, i), 4)],
                                      tmp[:, 512 * (bank % 2):512 * (bank % 2) + 256 * tn].rearrange("p (t h d) -> p t h d", h=4, d=HD),
                                      AX.X, add).then_inc(hs_ok, 1)
                lo(dve, 1, P_QKV + 1 + b, m, i)
            sums(0)
            with dve.Fori(0, 4) as i:
                sums(1, 1, i)
            dve.wait_ge(hs_sq, 1)
            dve.reciprocal(hs[:, :, :], hs[:, :, :]).then_inc(hs_rc, 1)

            def head_norm(t):
                row = qkv[:, t, 0:1280].rearrange("p (h d) -> p h d", d=HD)
                dve.tensor_tensor(row, row, hs[:, t, :].unsqueeze(2).to_broadcast([128, 20, HD]), mult).then_inc(nrm, 1)
                dve.wait_ge(nrm, 2 * t + 1)
                dve.tensor_tensor(row[:, 0:16], row[:, 0:16], gqk[:, 0, :].unsqueeze(1).to_broadcast([128, 16, HD]), mult)
                dve.tensor_tensor(row[:, 16:20], row[:, 16:20], gqk[:, 1, :].unsqueeze(1).to_broadcast([128, 4, HD]),
                                  mult).then_inc(nrm, 1)

            dve.wait_ge(hs_rc, 1)
            for t in range(6):
                head_norm(t)
            for s in range(2):
                lo(dve, s, P_WO)

            def merge(c, i=None):
                g, z = c % 4, c % 2
                b = S_BANK[z][0]
                dve.wait_ge(s_cp, at(c + 1, 8, i))
                if i is not None:
                    dve.sem_inc(hold_dve, 1)
                sv = sm[:, z, :].rearrange("p (e j n) -> p e j n", e=2, j=2)
                for e in range(2):
                    ins = dve.copy_predicated(sv[:, e], tb2[:, C_CUR:C_CUR + 128].bitcast(i32).unsqueeze(1).to_broadcast([128, 2, 128]),
                                              ps[:, b + e, 0:256].rearrange("p (j n) -> p j n", j=2))
                ins.then_inc(s_mrg, 1)
                dve.wait_ge(s_mrg, at(2 * c + 1, 16, i))
                dve.reduce_max(stt[:, 48 + 4 * z:52 + 4 * z], sm[:, z, :].rearrange("p (h n) -> p h n", h=4), AX.X).then_inc(s_mrg, 1)
                dve.wait_ge(s_mrg, at(2 * c + 2, 16, i))
                ns = nsk[:, 4 * g:4 * g + 4].rearrange("p (j e) -> p e j", e=2)
                nm = stt[:, 8 * z:8 * z + 4].rearrange("p (e j) -> p e j", e=2)
                dve.scalar_tensor_tensor(nm, stt[:, 48 + 4 * z:52 + 4 * z].rearrange("p (e j) -> p e j", e=2), -HD ** -0.5, ns,
                                         mult, ALU.min).then_inc(s_nm, 1)
                dve.wait_ge(s_nm, at(2 * c + 1, 16, i))
                dve.tensor_tensor(stt[:, 4 + 8 * z:8 + 8 * z].rearrange("p (e j) -> p e j", e=2), nm, ns, sub).then_inc(s_nm, 1)

            def normalise(c, i=None):
                z = c % 2
                dve.wait_ge(p_exp, at(c + 1, 8, i))
                dn = stt[:, 16 + 8 * z:20 + 8 * z]
                dve.tensor_tensor(dn, dn, stt[:, 20 + 8 * z:24 + 8 * z], add).then_inc(p_nrm, 1)
                dve.wait_ge(p_nrm, at(3 * c + 1, 24, i))
                dve.reciprocal(dn, dn).then_inc(p_nrm, 1)
                dve.wait_ge(p_nrm, at(3 * c + 2, 24, i))
                pv = pr[:, z, :].rearrange("p (h n) -> p h n", h=4)
                dve.tensor_tensor(pv, pv, dn.unsqueeze(2).to_broadcast([128, 4, 128]), mult).then_inc(p_nrm, 1)

            def mask(c, i=None):
                z = c % 2
                dve.wait_ge(p_t, at(c + 1, 8, i))
                if c >= 2:
                    dve.wait_ge(o_full, at(c - 1, 8, i))
                for dst, col in ((pc, C_CURT), (pp, C_PRVT)):
                    ins = dve.tensor_tensor(dst[:, z, :].rearrange("p (h n) -> p h n", h=4), ps[:, 7, :].rearrange("p (h n) -> p h n", h=4),
                                            tb2[:, col:col + 128].unsqueeze(1).to_broadcast([128, 4, 128]), mult)
                ins.then_inc(p_msk, 1)

            def step(c, i=None):
                mask(c, i)
                if i is not None or c + 1 < GROUPS_A:
                    normalise(c + 1, i)
                if i is not None or c + 3 < GROUPS_A:
                    merge(c + 3, i)

            dve.wait_ge(nsk_ok, 1)
            dve.wait_ge(w_used, 2 * P_WO)
            rotate(dve, t0, rope0, 0)
            for t in range(6, TT):
                head_norm(t)
            merge(0)
            merge(1)
            normalise(0)
            merge(2)
            for_steps(dve, step)

            dve.wait_ge(zero_a, 5)
            dve.wait_ge(qk_c, 27)
            dve.tensor_copy(qm[:, :, :].rearrange("p k (b n) -> p k b n", n=72)[:, :, :, 0:NT],
                            qTe[:, :, 64:128].rearrange("p k (b n) -> p k b n", n=NT)).then_inc(z_q, 1)
            dve.wait_ge(z_s, 2)
            tv = tmp[0:64, :]
            dve.tensor_tensor(tv.rearrange("p (a h n) -> p a h n", a=2, n=64), ps[0:64, 0:2, :].rearrange("p a (h n) -> p a h n", n=64),
                              tb2[0:64, C_BLC:C_BLC + 64].unsqueeze(1).unsqueeze(1).to_broadcast([64, 2, 8, 64]), mult).then_inc(z_n, 1)
            dve.wait_ge(z_n, 1)
            new = hs[0:64, :, :].rearrange("p t h -> p (t h)")[:, 0:128]
            dve.tensor_reduce(new.rearrange("p (h n) -> p h n", h=16), tv.rearrange("p (h b n) -> p h n b", h=16, b=NB), AX.X, add).then_inc(z_n, 1)
            dve.wait_ge(z_n, 2)
            dve.wait_ge(z_a, 1)
            dve.copy_predicated(ssc[:, :, 0:NT], tb2[0:64, C_NEW:C_NEW + NT].bitcast(i32).unsqueeze(1).to_broadcast([64, 16, NT]),
                                new.rearrange("p (h n) -> p h n", h=16)).then_inc(z_n, 1)
            dve.wait_ge(z_n, 3)
            dve.reduce_max(stt[0:64, 48:64], ssc[:, :, :], AX.X).then_inc(z_n, 1)
            dve.wait_ge(z_n, 4)
            mx = stt[0:64, 48:64].rearrange("p (e g j) -> p e g j", e=2, j=2)
            nm = stt[0:64, 0:16].rearrange("p (e g j) -> p e g j", e=2, j=2)
            sk = stt[0:64, 16:32].rearrange("p (e g j) -> p e g j", e=2, j=2)
            ns = nsk[0:64, :].rearrange("p (g j e) -> p e g j", e=2, j=2)
            for e in range(2):
                ins = dve.scalar_tensor_tensor(nm[:, e], mx[:, e], -HD ** -0.5, ns[:, e], mult, ALU.min)
            ins.then_inc(z_n, 1)
            dve.wait_ge(z_n, 5)
            for e in range(2):
                dve.tensor_tensor(sk[:, e], nm[:, e], ns[:, e], sub)
            dve.scalar_tensor_tensor(ssc[:, :, :], ssc[:, :, :], HD ** -0.5, stt[0:64, 0:16].unsqueeze(2).to_broadcast([64, 16, 128]),
                                     mult, add).then_inc(z_n, 1)
            dve.wait_ge(z_a, 3)
            dve.tensor_reduce(stt[0:64, 48:64], ssc[:, :, :], AX.X, add).then_inc(z_n, 1)
            dve.wait_ge(z_n, 7)
            dve.tensor_tensor(stt[0:64, 48:64], stt[0:64, 48:64], stt[0:64, 32:48], add).then_inc(z_n, 1)
            dve.wait_ge(z_n, 8)
            dve.reciprocal(stt[0:64, 48:64], stt[0:64, 48:64]).then_inc(z_n, 1)
            dve.wait_ge(z_n, 9)
            dve.tensor_tensor(ssc[:, :, :], ssc[:, :, :], stt[0:64, 48:64].unsqueeze(2).to_broadcast([64, 16, 128]), mult).then_inc(z_n, 1)
            dve.wait_ge(z_n, 10)
            dve.wait_ge(zero_a, 6)
            for b in range(NB):
                ins = dve.tensor_tensor(pn[:, :, 64 + NT * b:64 + NT * b + NT], ssc[:, :, 0:NT],
                                        tb2[0:64, C_BLC + 64 + NT * b:C_BLC + 64 + NT * b + NT].unsqueeze(1).to_broadcast([64, 16, NT]), mult)
            ins.then_inc(z_n, 1)
            dve.wait_ge(z_n, 11)
            dve.tensor_tensor(ssc[:, :, :], ssc[:, :, :], tb2[0:64, C_OLD:C_OLD + 128].unsqueeze(1).to_broadcast([64, 16, 128]), mult).then_inc(z_n, 1)

            for k in range(KT):
                dve.wait_ge(h_hi, 24 + k + 1)
                dve.tensor_tensor(hl[:, k, 0:SEQ].rearrange("p (t n) -> p t n", n=128), qkv[:, 0:8, 128 * k:128 * k + 128],
                                  hh[:, k, 0:SEQ].bitcast(f32).rearrange("p (t n) -> p t n", n=128), sub)
                dve.tensor_tensor(hl[:, k, SEQ:T], qkv[:, 8, 128 * k:128 * k + 64], hh[:, k, SEQ:T].bitcast(f32), sub).then_inc(h_lo, 1)
            for m in range(8):
                area = m % 2
                dve.wait_ge(w_used, 2 * P_WO + m + 1)
                for dst, src in zip(cut(x[:, m, :]), chunks(area)):
                    ins = dve.tensor_tensor(dst, dst, src, add)
                ins.then_inc(free[area], 1)
                lo(dve, m % 2, P_WO + 1 + m // 2)

        def keys_twice(pe, bank, keys):
            for g in range(NKV - 1):
                pe.transpose(ps[:, bank, 128 * g:128 * g + 128], keys[:, HD * g:HD * g + 2 * HD], idn[:, :])
            for e, g in ((0, NKV - 1), (1, 0)):
                ins = pe.matmul(ps[64 * e:64 * e + 64, bank, 384:512], keys[:, HD * g:HD * g + HD], idn[:, :], start=True, stop=True)
            return ins

        def attention_pe(pe, token_major):
            for a in (0, 1):
                pe.wait_ge(free[a], (A_WO, B_WO)[a])
            pe.wait_ge(halo, 4 * FI)
            token_major(P_QKV, None, first=16)
            pe.wait_ge(x_ss, 32)
            for t in range(TT):
                ins = pe.matmul(ps[:, 6, t:t + 1], ssum[:, TOK0[t]:TOK0[t] + 128], ones[:, 0:1], start=True, stop=True)
            ins.then_inc(stat, 1)
            with pe.Fori(0, 5) as i:
                token_major(P_QKV + 1, 8, 1, i)
            pe.wait_ge(tm_free, 70)
            pe.wait_ge(zero_a, 2)

            def transposes(n, j, i=None):
                if j == 0:
                    if n:
                        pe.wait_ge(rope, at(ROPE * n, 2 * ROPE, i))
                    else:
                        pe.wait_ge(rope0, ROPE)
                if n or j:
                    pe.wait_ge(qk_c, at(3 * n + j, 6, i))
                if j < 2:
                    for k in range(4):
                        ins = pe.transpose(ps[:, 0, k * 128:k * 128 + 128], qr[:, 128 * (4 * j + k):128 * (4 * j + k) + 128], idn[:, :])
                else:
                    ins = keys_twice(pe, 0, qr[:, 1024:1280])
                ins.then_inc(qk_t, 1)

            def scores(c, i=None):
                n, g = c // 4, c % 4
                qT = (qTe, qTo)[n % 2]
                if g == 0:
                    pe.wait_ge(qk_c, at(3 * n + 3, 6, i))
                if c >= 2:
                    pe.wait_ge(s_mrg, at(2 * (c - 2) + 1, 16, i))
                for old in range(2):
                    for j in range(2):
                        for e in range(2):
                            ins = pe.matmul(ps[:, S_BANK[c % 2][e], 256 * old + 128 * j:256 * old + 128 * j + 128],
                                            qT[64 * e:64 * e + 64, 2 * g + j, :],
                                            kT[64 * e:64 * e + 64, (n + old) % 2, (g - e) % NKV, :], start=True, stop=True)
                ins.then_inc(s_full, 1)

            def probs(c, i=None):
                pe.wait_ge(p_nrm, at(3 * c + 3, 24, i))
                if c:
                    pe.wait_ge(p_msk, at(c, 8, i))
                for h in range(4):
                    ins = pe.transpose(ps[:, 7, 128 * h:128 * h + 128], pr[:, c % 2, 128 * h:128 * h + 128], idn[:, :])
                ins.then_inc(p_t, 1)

            def output(c, i=None):
                n, g = c // 4, c % 4
                if g == 0:
                    pe.wait_ge(v_c, at(n + 1, 2, i))
                pe.wait_ge(p_msk, at(c + 1, 8, i))
                if c >= 2:
                    pe.wait_ge(o_ok, at(c - 1, 8, i))
                for e in range(2):
                    for old, src in ((0, pc), (1, pp)):
                        ins = pe.matmul(ps[64 * e:64 * e + 64, 1 + c % 2, 0:256], vb[:, (n + old) % 2, HD * g:HD * g + HD],
                                        src[:, c % 2, 256 * e:256 * e + 256], start=old == 0, stop=old == 1)
                ins.then_inc(o_full, 1)

            def step(c, i=None):
                probs(c, i)
                if i is not None or c + 3 < GROUPS_A:
                    scores(c + 3, i)
                piece = piece_at(c)
                if piece is not None and piece[0] <= 8:
                    transposes(*piece, i)
                output(c, i)

            for j in range(3):
                transposes(0, j)
            scores(0)
            scores(1)
            scores(2)
            transposes(1, 0)
            transposes(1, 1)
            for_steps(pe, step)

            pe.wait_ge(kc_in, 16)
            for b in range(NB):
                if b >= 4:
                    pe.wait_ge(kc_c, b - 3)
                keys_twice(pe, 3 + b % 4, kc[:, b, :]).then_inc(kc_t, 1)
            pe.wait_ge(kc_c, NB)
            pe.wait_ge(z_q, 1)
            for e in range(2):
                for g in range(NKV):
                    for j in range(2):
                        o = ps[0:64, 3 + 2 * e + g // 2, 256 * (g % 2) + 128 * j:256 * (g % 2) + 128 * j + 128]
                        for b in range(NB):
                            ins = pe.matmul(o, qm[64 * e:64 * e + 64, 2 * g + j, 64 * b:64 * b + 64],
                                            kcT[64 * e:64 * e + 64, b, (g - e) % NKV, :], start=b == 0, stop=b == NB - 1)
            ins.then_inc(z_s, 1)
            pe.wait_ge(qk_c, 27)
            pe.wait_ge(o_ok, GROUPS_A)
            for e in range(2):
                for g in range(NKV):
                    for j in range(2):
                        ins = pe.matmul(ps[0:64, e, 128 * g + 64 * j:128 * g + 64 * j + 64], qTe[64 * e:64 * e + 64, 2 * g + j, 64:128],
                                        kT[64 * e:64 * e + 64, 0, (g - e) % NKV, 64:128], start=True, stop=True)
            ins.then_inc(z_s, 1)
            pe.wait_ge(z_n, 12)
            for src, b0 in ((ssc, 3), (pn, 5)):
                for h in range(16):
                    ins = pe.transpose(ps[:, b0 + h // 8, 64 * (h % 8):64 * (h % 8) + 64], src[:, h, :], idn[0:64, 0:64])
                ins.then_inc(z_t, 1)
            pe.wait_ge(z_tc, 2)
            pe.wait_ge(kv_in, 16)
            for e in range(2):
                for g in range(NKV):
                    h = 8 * e + 2 * g
                    o = ps[64 * e:64 * e + 64, 2, 128 * g:128 * g + 128].rearrange("p (j n) -> p j n", j=2)
                    pe.matmul(o, vb[:, 0, HD * g:HD * g + HD], pnT[:, h:h + 2, :], start=True, stop=False, skip_group_check=True)
                    for b in range(NB):
                        ins = pe.matmul(o[:, :, NT * b:NT * b + NT], vc[:, b, HD * g:HD * g + HD], pcT[:, h:h + 2, NT * b:NT * b + NT],
                                        start=False, stop=True, skip_group_check=True)
            ins.then_inc(z_t, 1)

        def attention_out_pe(pe):
            pe.wait_ge(o_ok, GROUPS_A + 1)
            for m in range(8):
                area = m % 2
                pe.wait_ge(free[area], (A_WO, B_WO)[area] + m // 2)
                pe.wait_ge(w_lo, 2 * P_WO + m + 1)
                for k in range(KT):
                    if m == 0:
                        pe.wait_ge(h_lo, 24 + k + 1)
                    ins = rows(pe, area, m % 2, k, 128 * k, x_mov, k == 0, k == 7)
                ins.then_inc(w_used, 1)

        @block.sync
        def _(sp):
            sp.dma_start(tabs[:, :], table).then_inc(t_in, 16)
            xv = x_prompt[0].rearrange("(t p) n -> p t n", p=128)
            for i in range(4):
                sp.dma_start(xin[:, 2 * i:2 * i + 2, :], xv[:, 2 * i:2 * i + 2, :]).then_inc(x_in[i], 16)
            sp.dma_start(xin[0:64, 8, :], x_sample.rearrange("b t n -> (b t) n")).then_inc(x_in[4], 16)
            sp.dma_start(idn[:, :], table[:, C_ID:C_ID + 128]).then_inc(t_in, 16)
            sp.dma_start(vecs[0:16, 0, :], mix_norm_g.rearrange("l (k p) -> (l k) p", p=128)).then_inc(vec_in, 16)
            sp.dma_start(vecs[16:32, 0, :], ffn_norm_g.rearrange("l (k p) -> (l k) p", p=128)).then_inc(vec_in, 16)
            for L in range(2):
                for j in range(2):
                    sp.dma_start(vecs[44 * j:44 * j + 44, 1 + 2 * L, :],
                                 ffn_conv_w[L, j].rearrange("(k p) -> k p", p=128)).then_inc(vec_in, 16)
                sp.dma_start(vecs[0:44, 2 + 2 * L, :],
                             ffn_conv_w[L, 2].rearrange("(k p) -> k p", p=128)).then_inc(vec_in, 16)
                sp.dma_start(vecs[44:88, 2 + 2 * L, :],
                             ffn_conv_b[L].rearrange("(k p) -> k p", p=128)).then_inc(vec_in, 16)
            sp.dma_start(wsr[:, :, :], sgu_w_s[0].rearrange("g t s -> t g s")).then_inc(ws_in, 16)

            def v_pair(m=0, i=None):
                for s in range(2):
                    load(sp, sgu_w_in[0, 512 * s:512 * s + 512, bass.ds(at(SGU, 256 * m, i), 256)], s, 4, P_V, m, i)

            v_pair()
            with sp.Fori(1, 8) as i:
                v_pair(1, i)

            sp.wait_ge(ws8_ok, 2)
            sp.dma_start(bsb[:, :, :].rearrange("p g n -> p (g n)"),
                         sgu_b_s[0].rearrange("g n -> (g n)").partition_broadcast(128)).then_inc(bs_in, 16)

            def u_unit(s, c, p, m=0, i=None):
                load(sp, sgu_w_in[0, :, bass.ds(at(128 * c, 256 * m, i), 128)], s, 8, p, m, i)

            def ln_gains(s, c, m=0, i=None):
                col = bass.ds(at(128 * c, 256 * m, i), 128)
                sp.dma_start(lng[:, s, :], sgu_ln_g[0, col].partition_broadcast(128)).then_inc(ln_in[s], 16)
                sp.dma_start(lnb[:, s, :], sgu_ln_b[0, col].partition_broadcast(128)).then_inc(ln_in[s], 16)

            for s in range(2):
                u_unit(s, s, P_U)
                ln_gains(s, s)
            with sp.Fori(0, 7) as i:
                for s in range(2):
                    u_unit(s, 2 + s, P_U + 1, 1, i)
                    sp.wait_ge(ln, at(3 * s + 3, 6, i))
                    ln_gains(s, 2 + s, 1, i)

            def xm_load(m, i=None, c=0):
                col = bass.ds(at(128 * c, 128, i), 128)
                sp.dma_start(xm[:, 0:8, :], xv[:, :, col]).then_inc(xm_in, 16)
                sp.dma_start(xm[0:64, 8, :], x_sample.rearrange("b t n -> (b t) n")[:, col]).then_inc(xm_in, 16)

            def out_pair(c, p, m=0, i=None):
                for s in range(2):
                    load(sp, sgu_w_out[0, 1024 * s:1024 * s + 1024, bass.ds(at(128 * c, 128 * m, i), 128)],
                         s, 8, p, m, i)

            out_pair(0, P_OUT)
            xm_load(0)
            with sp.Fori(0, 7) as i:
                out_pair(1, P_OUT + 1, 1, i)
                sp.wait_ge(xm_used, at(1, 1, i))
                xm_load(1, i, 1)

            def ffn_loads(L):
                P = P_F[L]

                def up_pair(q, c, p, m=0, i=None):
                    for s in range(2):
                        load(sp, ffn_w_up[L, :, bass.ds(at(DFF * s + 128 * (2 * c + q), 256, i), 128)], s, 8, p, m, i)

                def down_pair(c, p, m=0, i=None):
                    for s in range(2):
                        load(sp, ffn_w_down[L, bass.ds(at(256 * c, 256, i), 256), 512 * s:512 * s + 512],
                             s, 2, p, m, i)

                def past(c, i=None):
                    if i is not None or L or c:
                        sp.wait_ge(past_t, at(FI * L + c, 1, i))
                    src = state_ffn_conv[L].rearrange("b r (z n) -> (b r) z n", z=2)
                    sp.dma_start(pst[:, :, :].rearrange("p (z q) n -> p z (q n)", z=2),
                                 src[:, :, bass.ds(at(256 * c, 256, i), 256)]).then_inc(past_in, 16)

                up_pair(0, 0, P)
                up_pair(1, 0, P + 1)
                past(0)
                with sp.Fori(0, FI - 2) as i:
                    up_pair(0, 1, P + 2, 3, i)
                    past(1, i)
                    down_pair(0, P + 3, 3, i)
                    up_pair(1, 1, P + 4, 3, i)
                up_pair(0, FI - 1, P + 3 * FI - 4)
                past(FI - 1)
                up_pair(1, FI - 1, P + 3 * FI - 3)
                down_pair(FI - 2, P + 3 * FI - 2)
                down_pair(FI - 1, P + 3 * FI - 1)

            ffn_loads(0)
            if STAGE > 1:
                attention_loads(sp)
                ffn_loads(1)
            for e in y_out:
                sp.wait_ge(e, 4 * 32)
            for e in v_out:
                sp.wait_ge(e, 8 * 16)
            if STAGE > 1:
                sp.wait_ge(kv_out, 4 * 16)
                sp.wait_ge(smp, 2 * NB * 16)
            sp.wait_ge(state_out, (2 if STAGE > 1 else 1) * 32 * FI)

        @block.gpsimd
        def _(pool):
            pool.memset(ones[:, :], 1.0).then_inc(ones_ok, 1)

            def sum_squares(n):
                for m in range(8):
                    for h in range(2):
                        half = ssum[:, h * (T // 2):(h + 1) * (T // 2)]
                        c = 16 * n + 2 * m + h
                        pool.wait_ge(x_sq, c + 1)
                        if m == 0:
                            if n:
                                pool.wait_ge(stat, STATS[n - 1])
                            pool.tensor_copy(half, square_slot(n, h)).then_inc(x_ss, 1)
                        else:
                            pool.wait_ge(x_ss, c - 1)
                            pool.tensor_tensor(half, half, square_slot(n, h), add).then_inc(x_ss, 1)

            def zero_halos(L):
                pool.memset(a_sb[:, :, 0:2], 0.0).then_inc(zero, 1)

            sum_squares(0)
            zero_halos(0)
            if STAGE > 1:
                sum_squares(1)
                attention_pool(pool)
                sum_squares(2)
                pool.wait_ge(h_lo, 40)
                zero_halos(1)

        @block.scalar
        def _(act):
            for t in range(TT):
                n = 128 if t < 8 else 64
                if t % 2 == 0:
                    act.wait_ge(x_in[t // 2], 16)
                if t:
                    act.wait_ge(sq_st, t)
                act.activation(junk[0:n, :], xin[0:n, t, :], ACT.Square, accum_out=ss[0:n, t:t + 1]).then_inc(sq_st, 1)
            act.wait_ge(sq_st, TT)
            act.wait_ge(eps_ok, 1)
            act.activation(rt[:, 0:8], ss[:, 0:8], ACT.Sqrt, scale=1.0 / D, bias=eps[:, :]).then_inc(rt_sq, 1)
            act.activation(rt[0:64, 8:9], ss[0:64, 8:9], ACT.Sqrt, scale=1.0 / D, bias=eps[0:64, :]).then_inc(rt_sq, 1)
            act.wait_ge(vec_t, 1)
            act.activation(gains[:, :], ps[:, 6, 0:32], ACT.Copy).then_inc(vec_ok, 1)
            act.activation(cw[:, :, :, :, :].rearrange("p l t r k -> p (l t r k)"), ps[:, 6, 32:384], ACT.Copy).then_inc(vec_ok, 1)
            act.wait_ge(t_in, 32)
            act.activation(selr[:, :], tabs[:, C_SEL:C_SEL + 128], ACT.Copy).then_inc(sel_ok, 1)
            act.wait_ge(ws_t, 1)
            act.activation(wth[:, :, :].rearrange("p (a g) n -> p a (g n)", a=2), ps[:, 3:5, :], ACT.Copy).then_inc(wt_hi, 1)
            for s in range(2):
                hi(act, s, P_V)
            act.wait_ge(vec_ok, 1)
            for k in range(KT):
                area = k % 2
                act.wait_ge(x_t, k + 1)
                for dst, src in zip(cut(hh[:, k, :]), chunks(area)):
                    ins = act.activation(dst, src, ACT.Identity, scale=gains[:, k:k + 1])
                ins.then_inc(h_hi, 1)

            def v_block(b, m=0, i=None):
                hi(act, 0, P_V + 1 + b, m, i)
                for t in range(0, TT, 2):
                    if t < 8:
                        act.wait_ge(tm_full, at(4 * b + t // 2 + 1, 4 * m, i))
                    else:
                        act.wait_ge(w_used, at(2 * (P_V + b) + 2, 2 * m, i))
                    tn = 2 if t < 8 else 1
                    for a in range(2):
                        src = ps[:, t // 2, 0:256 * tn].rearrange("p (t a n) -> p a t n", a=2, n=128)[:, a]
                        dst = v[:, bass.ds(at(2 * b + a, 2 * m, i), 1), t:t + tn, :].rearrange("p o t n -> p (o t) n")
                        ins = act.activation(dst, src, ACT.Gelu_apprx_tanh)
                    ins.then_inc(tm_free, 1)
                hi(act, 1, P_V + 1 + b, m, i)

            with act.Fori(0, 8) as i:
                v_block(0, 1, i)
            act.wait_ge(bna, TT)
            act.activation(rt[:, 0:TT], mv[:, :, 1], ACT.Sqrt, bias=eps[:, :]).then_inc(ln_sq, 1)

            def u_tile(n, i=None):
                s = n % 2
                act.wait_ge(ln, at(3 * n + 3, 6, i))
                if n:
                    act.wait_ge(mixed, at(n, 2, i))
                else:
                    act.wait_ge(w_used, 2 * P_U)
                act.activation(vnh[:, :, :], v[:, bass.ds(at(n, 2, i), 1), :, :].rearrange("p o t n -> p (o t) n"),
                               ACT.Copy).then_inc(vn_hi, 1)
                act.dma_start(v_rows[0].rearrange("b t n -> (b t) n")[:, bass.ds(at(128 * n, 256, i), 128)],
                              v[64:128, bass.ds(at(n, 2, i), 1), 8, :].rearrange("p o n -> p (o n)")).then_inc(v_out[s], 16)
                act.wait_ge(w_used, at(2 * P_U + n + 1, 2, i))
                if n:
                    act.wait_ge(gated, at(n, 2, i))
                for dst, src in zip(cut(u), chunks(0)):
                    ins = act.activation(dst, src, ACT.Gelu_apprx_tanh)
                ins.then_inc(free[0], 1)
                hi(act, s, P_U + 1 + n // 2, 1, i)

            u_tile(0)
            u_tile(1)
            with act.Fori(0, 7) as i:
                u_tile(2, i)
                u_tile(3, i)

            for c in range(16):
                if c == 0:
                    act.wait_ge(w_used, 2 * P_OUT)
                    act.wait_ge(gated, 16)
                act.activation(gh[:, c, :], gt[:, c, :], ACT.Copy).then_inc(g_hi, 1)

            def squares(n, m):
                for h in range(2):
                    c = 16 * n + 2 * m + h
                    if c:
                        act.wait_ge(x_ss, c if n == 0 or m == 0 else c - 1)
                    act.activation(square_slot(n, h), x[:, m, h * (T // 2):(h + 1) * (T // 2)], ACT.Square).then_inc(x_sq, 1)

            for m in range(8):
                hi_next = P_OUT + m + 1
                area = m % 2
                act.wait_ge(w_used, 2 * (P_OUT + m) + 2)
                for dst, src in zip(cut(x[:, m, :]), chunks(area)):
                    ins = act.activation(dst, src, ACT.Copy)
                ins.then_inc(free[area], 1)
                for s in range(2):
                    hi(act, s, hi_next)
                act.wait_ge(free[area], (A_O, B_O)[area] + m // 2 + 1)
                if m < 7:
                    squares(0, m)

            def split_hi(k, col):
                act.activation(hh[:, k, :], x[:, k, :], ACT.Identity, scale=gains[:, col + k:col + k + 1]).then_inc(h_hi, 1)

            def ffn(L):
                P, J = P_F[L], FT * L
                act.wait_ge(w_used, 2 * P)
                for k in range(KT):
                    split_hi(k, 16 + 8 * L)
                    if k == 3:
                        squares(2 * L, 7)
                act.wait_ge(stat, STATS[2 * L])
                for dst, src in zip(cut(rbc), chunks(1)):
                    ins = act.activation(dst, src, ACT.Sqrt, scale=1.0 / D, bias=eps[:, :])
                ins.then_inc(rb_sq, 1)

                def conv_start(q, c, i=None):
                    j = J + 2 * c + q
                    for z, dst in ((0, cg), (1, cv)):
                        act.wait_ge(halo, at(2 * j + z + 1, 4, i))
                        if z == 1 and (i is not None or j):
                            act.wait_ge(mtok, at(j, 2, i))
                        if i is not None:
                            act.sem_inc(hold_act, 1)
                        k = bass.ds(at(FT * z + 2 * c + q, 2, i), 1)
                        act.activation(dst[:, 0:CW], a_sb[:, z, 2:2 + CW], ACT.Identity, scale=cw[:, L, 1, 0, k],
                                       bias=cw[:, L, 1, 1, k]).then_inc(conv0, 1)

                def silu_hi(q, c, m=0, i=None):
                    j = J + 2 * c + q
                    act.wait_ge(conv, at(4 * j + 2, 8, i))
                    if i is not None or j:
                        act.wait_ge(mtok, at(j, 2, i))
                    act.activation(sg[:, 0:CW], cg[:, 0:CW], ACT.Silu).then_inc(silu, 1)

                def act_hi(q, c, i=None, dst=None):
                    j = J + 2 * c + q
                    act.wait_ge(mtok, at(j + 1, 2, i))
                    act.activation(fh[:, q, :] if dst is None else dst, mt[:, :], ACT.Copy).then_inc(f_hi, 1)

                def state(c, i=None):
                    n = FI * L + c
                    act.wait_ge(state_t, at(n + 1, 1, i))
                    act.activation(sto[:, :, :].rearrange("p z n -> p (z n)"), ps[0:18, 7, :], ACT.Copy).then_inc(state_o, 1)
                    act.wait_ge(state_o, at(n + 1, 1, i))
                    col = bass.ds(at(256 * c, 256, i), 256)
                    st = sto[:, :, :].rearrange("p (z q) n -> p z (q n)", z=2)
                    act.dma_start(conv_prompt[L, 0].rearrange("r (z n) -> r z n", z=2)[:, :, col], st[0:2]).then_inc(state_out, 16)
                    act.dma_start(conv_sample[L].rearrange("b r (z n) -> (b r) z n", z=2)[:, :, col], st[2:18]).then_inc(state_out, 16)

                def state_stored(c, i=None):
                    act.wait_ge(state_out, at(32 * (FI * L + c + 1), 32, i))

                hi(act, 0, P + 1)
                hi(act, 1, P + 1)
                conv_start(0, 0)
                silu_hi(0, 0)
                act_hi(0, 0)
                hi(act, 0, P + 2)
                hi(act, 1, P + 2)
                conv_start(1, 0)
                silu_hi(1, 0)
                act_hi(1, 0)
                with act.Fori(0, FI - 2) as i:
                    hi(act, 0, P + 3, 3, i)
                    state(0, i)
                    hi(act, 1, P + 3, 3, i)
                    conv_start(0, 1, i)
                    silu_hi(0, 1, 3, i)
                    hi(act, 0, P + 4, 3, i)
                    hi(act, 1, P + 4, 3, i)
                    act_hi(0, 1, i)
                    hi(act, 0, P + 5, 3, i)
                    hi(act, 1, P + 5, 3, i)
                    conv_start(1, 1, i)
                    silu_hi(1, 1, 3, i)
                    act_hi(1, 1, i)
                    state_stored(0, i)
                last, c = P + 3 * FI, FI - 1
                hi(act, 0, last - 3)
                state(c - 1)
                hi(act, 1, last - 3)
                conv_start(0, c)
                silu_hi(0, c)
                act_hi(0, c, dst=fh[:, 2, :])
                hi(act, 0, last - 2)
                hi(act, 1, last - 2)
                conv_start(1, c)
                silu_hi(1, c)
                act_hi(1, c, dst=fhx[:, 0, :])
                hi(act, 0, last - 1)
                hi(act, 1, last - 1)
                state_stored(c - 1)
                state(c)
                if L == 0:
                    for m in range(8):
                        act.wait_ge(free[m % 2], (A_F, B_F)[m % 2][0] + 62 + m // 2 + 1)
                        split_hi(m, 8)
                        if m == 4:
                            hi(act, 0, last)
                        squares(1, m)
                    hi(act, 1, last)

            ffn(0)
            if STAGE > 1:
                attention_act(act, squares)
                ffn(1)
            for m in range(8):
                act.wait_ge(y_c, m + 1)
                act.dma_start(y_prompt[0].rearrange("(t p) n -> p t n", p=128)[:, :, 128 * m:128 * m + 128],
                              yst[:, m % 2, 0:8, :]).then_inc(y_out[m % 2], 16)
                act.dma_start(y_sample.rearrange("b t n -> (b t) n")[:, 128 * m:128 * m + 128],
                              yst[0:64, m % 2, 8, :]).then_inc(y_out[m % 2], 16)

        @block.vector
        def _(dve):
            dve.memset(eps[:, :], EPS).then_inc(eps_ok, 1)
            for area in range(2):
                dve.sem_inc(free[area], 1)
            dve.wait_ge(ws_in, 16)
            dve.wait_ge(t_in, 32)
            dve.tensor_tensor(wsr[:, :, :], wsr[:, :, :], tabs[:, C_CUR:C_CUR + 128].unsqueeze(1).to_broadcast([128, GROUPS, 128]),
                              mult).then_inc(ws_msk, 1)
            dve.wait_ge(rt_sq, 2)
            dve.reciprocal(rt[:, 0:8], rt[:, 0:8]).then_inc(rt_rc, 1)
            dve.reciprocal(rt[0:64, 8:9], rt[0:64, 8:9]).then_inc(rt_rc, 1)
            dve.wait_ge(rt_rc, 2)
            for t in range(TT):
                n = 128 if t < 8 else 64
                dve.tensor_scalar(xin[0:n, t, :], xin[0:n, t, :], rt[0:n, t:t + 1], None, mult).then_inc(xn, 1)
            dve.wait_ge(wt_hi, 1)
            dve.tensor_tensor(wtl[:, :, :].rearrange("p (a g) n -> p a (g n)", a=2), ps[:, 3:5, :],
                              wth[:, :, :].bitcast(f32).rearrange("p (a g) n -> p a (g n)", a=2), sub).then_inc(wt_lo, 1)
            for s in range(2):
                lo(dve, s, P_V)
            for n, (dst, bank) in enumerate(((wsh, 7), (wsl, 6))):
                dve.wait_ge(ws8_t, n + 1)
                dve.tensor_tensor(dst[:, :, :], ps[:, bank, :].rearrange("p (g n) -> p g n", g=GROUPS),
                                  tabs[:, C_BLK:C_BLK + 64].unsqueeze(1).to_broadcast([128, GROUPS, 64]), mult).then_inc(ws8_ok, 1)
            dve.wait_ge(vec_ok, 1)
            for k in range(KT):
                area = k % 2
                dve.wait_ge(h_hi, k + 1)
                for dst, hi_, src in zip(cut(hl[:, k, :]), cut(hh[:, k, :].bitcast(f32)), chunks(area)):
                    ins = dve.scalar_tensor_tensor(dst, src, gains[:, k:k + 1], hi_, mult, sub)
                ins.then_inc(h_lo, 1)

            with dve.Fori(0, 8) as i:
                lo(dve, 0, P_V + 1, 1, i)
                for t in range(TT):
                    if t % 2 == 0:
                        dve.wait_ge(tm_free, at(t // 2 + 1, 5, i))
                    dve.bn_stats(bst[:, t, bass.ds(i, 1), :].rearrange("p o n -> p (o n)"),
                                 v[:, bass.ds(at(0, 2, i), 2), t, :]).then_inc(bn, 1)
                lo(dve, 1, P_V + 1, 1, i)
            dve.wait_ge(bn, 8 * TT)
            for t in range(TT):
                dve.bn_aggr(mv[:, t, :], bst[:, t, :, :].rearrange("p b n -> p (b n)")).then_inc(bna, 1)
            dve.wait_ge(ln_sq, 1)
            dve.reciprocal(rt[:, 0:TT], rt[:, 0:TT]).then_inc(ln_rc, 1)

            def layer_norm(n, i=None):
                s = n % 2
                vt = v[:, bass.ds(at(n, 2, i), 1), :, :].rearrange("p o t n -> p (o t) n")
                for t in range(TT):
                    row = v[:, bass.ds(at(n, 2, i), 1), t, :].rearrange("p o n -> p (o n)")
                    ins = dve.tensor_scalar(row, row, mv[:, t, 0:1], rt[:, t:t + 1], sub, mult)
                ins.then_inc(ln, 1)
                dve.wait_ge(ln_in[s], at(32 * (n // 2 + 1), 32, i))
                dve.wait_ge(ln, at(3 * n + 1, 6, i))
                dve.tensor_tensor(vt, vt, lng[:, s, :].unsqueeze(1).to_broadcast([128, TT, 128]), mult).then_inc(ln, 1)
                dve.wait_ge(ln, at(3 * n + 2, 6, i))
                dve.tensor_tensor(vt, vt, lnb[:, s, :].unsqueeze(1).to_broadcast([128, TT, 128]), add).then_inc(ln, 1)

            def v_lo(n, i=None):
                vt = v[:, bass.ds(at(n, 2, i), 1), :, :].rearrange("p o t n -> p (o t) n")
                dve.wait_ge(vn_hi, at(n + 1, 2, i))
                dve.tensor_tensor(vnl[:, :, :], vt, vnh[:, :, :].bitcast(f32), sub).then_inc(vn_lo, 1)
                lo(dve, n % 2, P_U + 1 + n // 2, 1, i)

            def gating(n, i=None):
                s = n % 2
                dve.wait_ge(mixed, at(n + 1, 2, i))
                dve.wait_ge(v_out[s], at(16 * (n // 2 + 1), 16, i))
                g = bsb[:, bass.ds(at(n // 2, 1, i), 1), :].rearrange("p o n -> p (o n)")
                out = gt[:, bass.ds(at(n, 2, i), 1), :].rearrange("p o n -> p (o n)")
                b = BANK[1]
                dve.tensor_tensor(out[:, 0:768].rearrange("p (a c n) -> p a c n", a=2, n=128),
                                  ps[:, b:b + 2, 0:384].rearrange("p a (c n) -> p a c n", n=128),
                                  g.unsqueeze(1).unsqueeze(1).to_broadcast([128, 2, 3, 128]), add)
                dve.tensor_tensor(out[:, 768:1024].rearrange("p (c n) -> p c n", n=128),
                                  ps[:, b + 2, 0:256].rearrange("p (c n) -> p c n", n=128),
                                  g.unsqueeze(1).to_broadcast([128, 2, 128]), add)
                dve.tensor_tensor(out[:, 1024:T].rearrange("p (c n) -> p c n", n=NT),
                                  ps[:, b + 2, 256:320].rearrange("p (c n) -> p c n", n=NT),
                                  g[:, 0:NT].unsqueeze(1).to_broadcast([128, NB, NT]), add).then_inc(free[1], 1)
                dve.wait_ge(free[1], at(B_U + n + 1, 2, i))
                dve.wait_ge(free[0], at(A_U + n + 1, 2, i))
                dve.tensor_tensor(out, out, u[:, :], mult).then_inc(gated, 1)

            dve.wait_ge(ln_rc, 1)
            dve.wait_ge(bs_in, 16)
            layer_norm(0)
            with dve.Fori(0, 7) as i:
                for n in range(2):
                    v_lo(n, i)
                    layer_norm(n + 1, i)
                    gating(n, i)
            v_lo(14)
            layer_norm(15)
            gating(14)
            v_lo(15)
            gating(15)

            for c in range(16):
                dve.wait_ge(g_hi, c + 1)
                dve.tensor_tensor(gl[:, c, :], gt[:, c, :], gh[:, c, :].bitcast(f32), sub).then_inc(g_lo, 1)
            for m in range(8):
                for s in range(2):
                    lo(dve, s, P_OUT + m + 1)

            def split_lo(n, col, k):
                dve.wait_ge(h_hi, 8 * n + k + 1)
                dve.scalar_tensor_tensor(hl[:, k, :], x[:, k, :], gains[:, col + k:col + k + 1],
                                         hh[:, k, :].bitcast(f32), mult, sub).then_inc(h_lo, 1)

            def ffn(L):
                P, J = P_F[L], FT * L
                FA, FB = A_F[L], B_F[L]
                for k in range(KT):
                    split_lo(1 if L == 0 else 4, 16 + 8 * L, k)
                lo(dve, 0, P + 1)
                dve.wait_ge(rb_sq, L + 1)
                dve.reciprocal(rbc[:, :], rbc[:, :]).then_inc(rb_ok, 1)
                dve.wait_ge(rb_ok, L + 1)
                dve.wait_ge(zero, L + 1)

                def take(z, q, area, n_area, unit, mu, c, i=None):
                    j = J + 2 * c + q
                    dve.wait_ge(w_used, at(unit + 1, mu, i))
                    b = BANK[area]
                    dve.tensor_tensor(a_sb[:, z, 2:770].rearrange("p (c n) -> p c n", c=2), ps[:, b:b + 2, 0:384],
                                      rbc[:, 0:768].rearrange("p (c n) -> p c n", c=2), mult)
                    dve.tensor_tensor(a_sb[:, z, 770:1026], ps[:, b + 2, 0:256], rbc[:, 768:1024], mult)
                    smp = a_sb[:, z, 1026:1026 + NB * STEP].rearrange("p (b n) -> p b n", n=STEP)
                    dve.tensor_tensor(smp[:, :, 2:STEP], ps[:, b + 2, 256:320].rearrange("p (b n) -> p b n", n=NT),
                                      rbc[:, 1024:T].rearrange("p (b n) -> p b n", n=NT), mult).then_inc(free[area], 1)
                    dve.wait_ge(past_t, at(FI * L + c + 1, 1, i))
                    col = (2 * z + q) * 16
                    dve.tensor_copy(smp[:, :, 0:2], ps[:, 6, col:col + 16].rearrange("p (b r) -> p b r", r=2)).then_inc(halo, 1)
                    if i is not None or J + c:
                        dve.wait_ge(state_t, at(FI * L + c, 1, i))
                    dve.wait_ge(free[area], at(n_area + 1, 6, i))
                    last = a_sb[:, z, 1024:1024 + 9 * STEP].rearrange("p (g n) -> p g n", n=STEP)[:, :, 0:2]
                    dve.tensor_copy(stc[:, 2 * z + q, :].rearrange("p (g n) -> p g n", n=2), last).then_inc(state_c, 1)
                    dve.wait_ge(halo, at(2 * j + z + 1, 4, i))

                def conv_tap(q, c, z, r, i=None):
                    j = J + 2 * c + q
                    dst = (cg, cv)[z]
                    if r == 1:
                        dve.wait_ge(conv0, at(2 * j + z + 1, 4, i))
                    else:
                        dve.wait_ge(conv, at(4 * j + 2 * z + 1, 8, i))
                    dve.scalar_tensor_tensor(dst[:, 0:CW], a_sb[:, z, r:r + CW], cw[:, L, 0, r, bass.ds(at(FT * z + 2 * c + q, 2, i), 1)],
                                             dst[:, 0:CW], mult, add).then_inc(conv, 1)

                def gate_value(q, c, i=None):
                    j = J + 2 * c + q
                    dve.wait_ge(conv, at(4 * j + 4, 8, i))
                    dve.wait_ge(silu, at(j + 1, 2, i))
                    if i is not None or j:
                        dve.wait_ge(f_lo, at(j, 2, i))
                    dve.tensor_tensor(mt[:, 0:SEQ], sg[:, 0:SEQ], cv[:, 0:SEQ], mult)
                    dve.tensor_tensor(mt[:, SEQ:T].rearrange("p (b n) -> p b n", n=NT),
                                      sg[:, SEQ + 2:SEQ + 2 + NB * STEP].rearrange("p (b n) -> p b n", n=STEP)[:, :, 0:NT],
                                      cv[:, SEQ + 2:SEQ + 2 + NB * STEP].rearrange("p (b n) -> p b n", n=STEP)[:, :, 0:NT],
                                      mult).then_inc(mtok, 1)

                def convolve(q, c, i=None):
                    for z, r in ((0, 1), (0, 0), (1, 1), (1, 0)):
                        conv_tap(q, c, z, r, i)
                    gate_value(q, c, i)

                def act_lo(q, c, i=None, dst=None, high=None):
                    j = J + 2 * c + q
                    dve.wait_ge(f_hi, at(j + 1, 2, i))
                    dve.tensor_tensor(fl[:, q, :] if dst is None else dst, mt[:, :],
                                      (fh[:, q, :] if high is None else high).bitcast(f32), sub).then_inc(f_lo, 1)

                def add_down(m, n_down, unit, n_area, i=None):
                    area = m % 2
                    if m in (3, 7):
                        dve.wait_ge(w_used, at(unit + m // 4 + 1, 6, i))
                    else:
                        dve.wait_ge(down, at(n_down + (m if m < 3 else m - 1) + 1, 6, i))
                    for dst, src in zip(cut(x[:, m, :]), chunks(area)):
                        ins = dve.tensor_tensor(dst, dst, src, add)
                    ins.then_inc(free[area], 1)

                take(0, 0, 0, FA, 2 * P, 6, 0)
                lo(dve, 1, P + 1)
                take(1, 0, 1, FB, 2 * P + 1, 6, 0)
                convolve(0, 0)
                act_lo(0, 0)
                lo(dve, 0, P + 2)
                take(0, 1, 0, FA + 1, 2 * P + 2, 6, 0)
                lo(dve, 1, P + 2)
                take(1, 1, 1, FB + 1, 2 * P + 3, 6, 0)
                convolve(1, 0)
                act_lo(1, 0)
                U = 2 * (P + 2)
                DN = 66 * L
                with dve.Fori(0, FI - 2) as i:
                    lo(dve, 0, P + 3, 3, i)
                    take(0, 0, 0, FA + 2, U, 6, 1, i)
                    lo(dve, 1, P + 3, 3, i)
                    take(1, 0, 1, FB + 2, U + 1, 6, 1, i)
                    add_down(0, DN, U + 2, None, i)
                    conv_tap(0, 1, 0, 1, i)
                    add_down(1, DN, U + 2, None, i)
                    conv_tap(0, 1, 0, 0, i)
                    add_down(2, DN, U + 2, None, i)
                    conv_tap(0, 1, 1, 1, i)
                    add_down(3, DN, U + 2, None, i)
                    lo(dve, 0, P + 4, 3, i)
                    add_down(4, DN, U + 2, None, i)
                    conv_tap(0, 1, 1, 0, i)
                    add_down(5, DN, U + 2, None, i)
                    gate_value(0, 1, i)
                    add_down(6, DN, U + 2, None, i)
                    add_down(7, DN, U + 2, None, i)
                    lo(dve, 1, P + 4, 3, i)
                    act_lo(0, 1, i)
                    lo(dve, 0, P + 5, 3, i)
                    take(0, 1, 0, FA + 7, U + 4, 6, 1, i)
                    lo(dve, 1, P + 5, 3, i)
                    take(1, 1, 1, FB + 7, U + 5, 6, 1, i)
                    convolve(1, 1, i)
                    act_lo(1, 1, i)
                last, c, r = P + 3 * FI, FI - 1, 6 * (FI - 2)
                lo(dve, 0, last - 3)
                take(0, 0, 0, FA + 2 + r, 2 * (last - 4), 6, c)
                lo(dve, 1, last - 3)
                take(1, 0, 1, FB + 2 + r, 2 * (last - 4) + 1, 6, c)
                convolve(0, c)
                act_lo(0, c, dst=fl[:, 2, :], high=fh[:, 2, :])
                lo(dve, 0, last - 2)
                take(0, 1, 0, FA + 3 + r, 2 * (last - 3), 6, c)
                lo(dve, 1, last - 2)
                take(1, 1, 1, FB + 3 + r, 2 * (last - 3) + 1, 6, c)
                for m in range(8):
                    add_down(m, DN + r, 2 * (last - 2), None)
                    if m in (0, 1):
                        conv_tap(1, c, 0, 1 - m)
                    if m in (2, 4):
                        conv_tap(1, c, 1, (4 - m) // 2)
                    if m == 5:
                        gate_value(1, c)
                    if m == 6:
                        act_lo(1, c, dst=flx[:, 0, :], high=fhx[:, 0, :])
                lo(dve, 0, last - 1)
                lo(dve, 1, last - 1)
                for m in range(8):
                    add_down(m, DN + 6 * (FI - 1), 2 * (last - 1), None)
                    if L == 0 and m:
                        split_lo(2, 8, m - 1)
                    if L == 0 and m == 6:
                        lo(dve, 0, last)
                if L == 0:
                    split_lo(2, 8, 7)
                    lo(dve, 1, last)

            ffn(0)
            if STAGE > 1:
                attention_dve(dve)
                ffn(1)
            for m in range(8):
                b = BANK[m % 2]
                dve.wait_ge(y_t, m + 1)
                if m >= 2:
                    dve.wait_ge(y_out[m % 2], 32 * (m // 2))
                y = yst[:, m % 2, :, :]
                dve.tensor_copy(y[:, 0:6, :].rearrange("p (a c) n -> p a (c n)", a=2), ps[:, b:b + 2, 0:384])
                dve.tensor_copy(y[:, 6:8, :].rearrange("p c n -> p (c n)"), ps[:, b + 2, 0:256])
                dve.tensor_copy(y[0:64, 8, :], ps[0:64, b + 2, 256:384]).then_inc(y_c, 1)

        @block.tensor
        def _(pe):
            pe.wait_ge(t_in, 32)
            pe.wait_ge(vec_in, 160)
            pe.transpose(ps[:, 6, 0:32], vecs[0:32, 0, :], idn[0:32, 0:32])
            for n in range(4):
                ins = pe.transpose(ps[:, 6, 32 + 88 * n:120 + 88 * n], vecs[0:88, 1 + n, :], idn[0:88, 0:88])
            ins.then_inc(vec_t, 1)
            pe.wait_ge(ws_msk, 1)
            for g in range(GROUPS):
                ins = pe.transpose(ps[:, 3 + g // 4, (g % 4) * 128:(g % 4) * 128 + 128], wsr[:, g, :], idn[:, :])
            ins.then_inc(ws_t, 1)
            pe.wait_ge(sel_ok, 1)
            pe.wait_ge(wt_hi, 1)
            pe.wait_ge(vec_ok, 2)
            for src, bank, done in ((wth, 7, None), (wtl, 6, wt_lo)):
                if done is not None:
                    pe.wait_ge(done, 1)
                for g in range(GROUPS):
                    ins = pe.matmul(ps[:, bank, 64 * g:64 * g + 64], selr[:, :],
                                    src[:, g, 0:NT].unsqueeze(1).to_broadcast([128, NB, NT]), start=True, stop=True)
                ins.then_inc(ws8_t, 1)
            pe.wait_ge(xn, TT)
            for k in range(KT):
                if k == 1:
                    pe.wait_ge(wt_lo, 1)
                if k >= 2:
                    pe.wait_ge(h_lo, k - 1)
                for t in range(TT):
                    n = 128 if t < 8 else 64
                    ins = pe.transpose(ps[:, BANK[k % 2] + t // 3, (t % 3) * 128:(t % 3) * 128 + n],
                                       xin[0:n, t, 128 * k:128 * k + 128], idn[0:n, 0:n])
                ins.then_inc(x_t, 1)

            def token_major(p0, n0, m=0, i=None, first=None):
                for s in range(2):
                    pe.wait_ge(w_lo, at(2 * p0 + s + 1, 2 * m, i))
                    order = [(k, t) for k in range(4) for t in range(TT)] if s == 0 else \
                            [(k, t) for t in range(TT) for k in range(4)]
                    for k, t in order:
                        if first is not None and s == 0 and t == 0:
                            pe.wait_ge(h_lo, first + (k + 1 if k < 3 else KT))
                        if s == 0 and k == 0 and t % 2 == 0 and n0 is not None:
                            pe.wait_ge(tm_free, at(5 * n0 + t // 2 + 1, 5 * m, i))
                        o = ps[:, t // 2, (t % 2) * 256:(t % 2) * 256 + 256]
                        for n, (a, w) in enumerate(((hh, wh), (hh, wl), (hl, wh))):
                            ins = pe.matmul(o, a[:, 4 * s + k, TOK0[t]:TOK0[t] + 128], w[:, s, 256 * k:256 * k + 256],
                                            start=s == 0 and k == 0 and n == 0 and t % 2 == 0,
                                            stop=s == 1 and k == 3 and n == 2, skip_group_check=True)
                        if s == 1 and k == 3 and t < 8 and t % 2:
                            ins.then_inc(tm_full, 1)
                    ins.then_inc(w_used, 1)

            pe.wait_ge(h_lo, KT)
            pe.wait_ge(ws8_ok, 2)
            token_major(P_V, None)
            with pe.Fori(0, 7) as i:
                token_major(P_V + 1, 0, 1, i)

            pe.wait_ge(tm_free, 40)
            with pe.Fori(0, 8) as i:
                for s in range(2):
                    if s:
                        pe.wait_ge(free[0], at(A_U + 1, 2, i))
                    else:
                        pe.wait_ge(free[0], at(A_U, 2, i))
                    pe.wait_ge(w_lo, at(2 * P_U + s + 1, 2, i))
                    for k in range(KT):
                        ins = rows(pe, 0, s, k, 128 * k, x_mov, k == 0, k == 7)
                    ins.then_inc(w_used, 1)
                    pe.wait_ge(vn_lo, at(s + 1, 2, i))
                    pe.wait_ge(free[1], at(B_U + s, 2, i))
                    for t in range(TT):
                        n = 128 if t < 8 else 64
                        gi = bass.ds(i, 1)
                        src = (wth, wtl) if t < 8 else (wsh, wsl)
                        o = ps[:, 3 + t // 3, (t % 3) * 128:(t % 3) * 128 + n]
                        for r, (a, w) in enumerate(((vnh, src[0]), (vnh, src[1]), (vnl, src[0]))):
                            ins = pe.matmul(o, a[:, t, :], w[:, gi, :].rearrange("p o n -> p (o n)"),
                                            start=r == 0, stop=r == 2)
                    ins.then_inc(mixed, 1)

            for m in range(8):
                area = m % 2
                pe.wait_ge(free[area], (A_O, B_O)[area] + m // 2)
                pe.wait_ge(xm_in, 32 * (m + 1))
                for t in range(TT):
                    n = 128 if t < 8 else 64
                    ins = pe.matmul(ps[:, BANK[area] + t // 3, (t % 3) * 128:(t % 3) * 128 + n], xm[0:n, t, :],
                                    idn[0:n, 0:n], start=t % 3 == 0, stop=False, skip_group_check=True)
                ins.then_inc(xm_used, 1)
                for s in range(2):
                    pe.wait_ge(w_lo, 2 * (P_OUT + m) + s + 1)
                    for k in range(8):
                        if m == 0:
                            pe.wait_ge(g_lo, 8 * s + k + 1)
                        ins = rows(pe, area, s, 8 * s + k, 128 * k, g_mov, False, s == 1 and k == 7)
                    ins.then_inc(w_used, 1)

            def ffn(L):
                P, J = P_F[L], FT * L
                FA, FB = A_F[L], B_F[L]

                def past(c, i=None):
                    n = FI * L + c
                    pe.wait_ge(past_in, at(16 * (n + 1), 16, i))
                    if i is not None or n:
                        pe.wait_ge(halo, at(4 * n, 4, i))
                    for z in range(4):
                        ins = pe.matmul(ps[:, 6, 16 * z:16 * z + 16], pst[:, z, :], idn[0:16, 0:16], start=True, stop=True)
                    ins.then_inc(past_t, 1)

                def state(c, i=None):
                    n = FI * L + c
                    pe.wait_ge(state_c, at(4 * (n + 1), 4, i))
                    for z in range(4):
                        ins = pe.transpose(ps[0:18, 7, 128 * z:128 * z + 128], stc[:, z, :], idn[:, :])
                    ins.then_inc(state_t, 1)

                def up(s, area, n_area, p, m=0, i=None, inside=None, first=False):
                    pe.wait_ge(free[area], at(n_area, 6, i))
                    pe.wait_ge(w_lo, at(2 * p + s + 1, 2 * m, i))
                    for k in range(KT):
                        if first:
                            pe.wait_ge(h_lo, 8 * (1 if L == 0 else 4) + k + 1)
                        if k == 6 and inside is not None:
                            inside()
                        ins = rows(pe, area, s, k, 128 * k, x_mov, k == 0, k == 7)
                    ins.then_inc(w_used, 1)

                def down_proj(na, nb, p, m_=0, i=None, last=False):
                    for m in range(8):
                        area, s = m % 2, m // 4
                        pe.wait_ge(free[area], at((na, nb)[area] + m // 2, 6, i))
                        if m % 4 == 0:
                            pe.wait_ge(w_lo, at(2 * p + s + 1, 2 * m_, i))
                        for k in range(2):
                            mov, slot = (((fh, fl), 2), ((fhx, flx), 0))[k] if last else ((fh, fl), k)
                            ins = rows(pe, area, s, slot, 512 * k + 128 * (m % 4), mov, k == 0, k == 1)
                        ins.then_inc(w_used if m % 4 == 3 else down, 1)

                up(0, 0, FA, P, inside=lambda: past(0), first=True)
                pe.wait_ge(x_ss, 16 * (L + 1 + (L == 1)))
                pe.wait_ge(free[1], FB)
                pe.wait_ge(ones_ok, 1)
                for c, (c0, cn) in enumerate(CH):
                    ins = pe.matmul(ps[:, 3 + c, 0:cn], ones[:, :], ssum[:, c0:c0 + cn], start=True, stop=True)
                ins.then_inc(stat, 1)
                pe.wait_ge(rb_sq, L + 1)
                up(1, 1, FB, P)
                up(0, 0, FA + 1, P + 1)
                up(1, 1, FB + 1, P + 1)
                with pe.Fori(0, FI - 2) as i:
                    def edge():
                        past(1, i)
                        state(0, i)
                    up(0, 0, FA + 2, P + 2, 3, i, inside=edge)
                    up(1, 1, FB + 2, P + 2, 3, i)
                    pe.wait_ge(f_lo, at(J + 2, 2, i))
                    down_proj(FA + 3, FB + 3, P + 3, 3, i)
                    up(0, 0, FA + 7, P + 4, 3, i)
                    up(1, 1, FB + 7, P + 4, 3, i)
                    pe.wait_ge(state_o, at(FI * L + 1, 1, i))
                c, r, last = FI - 1, 6 * (FI - 2), P + 3 * FI

                def last_edge():
                    past(c)
                    state(c - 1)
                up(0, 0, FA + 2 + r, last - 4, inside=last_edge)
                up(1, 1, FB + 2 + r, last - 4)
                up(0, 0, FA + 3 + r, last - 3)
                up(1, 1, FB + 3 + r, last - 3)
                pe.wait_ge(f_lo, J + 2 * c)
                down_proj(FA + 4 + r, FB + 4 + r, last - 2)
                pe.wait_ge(state_o, FI * L + c)
                state(c)
                pe.wait_ge(f_lo, J + 2 * FI)
                down_proj(FA + 8 + r, FB + 8 + r, last - 1, last=True)

            ffn(0)
            if STAGE > 1:
                attention_pe(pe, token_major)
                attention_out_pe(pe)
                ffn(1)
            for m in range(8):
                area = m % 2
                n = (A_END, B_END)[area] - 3 + m // 2
                pe.wait_ge(free[area], n)
                if m == 0:
                    for a in (0, 1):
                        pe.wait_ge(free[a], (A_END, B_END)[a])
                if m >= 2:
                    pe.wait_ge(y_c, m - 1)
                for t in range(TT):
                    w = 128 if t < 8 else 64
                    ins = pe.transpose(ps[0:w, BANK[area] + t // 3, (t % 3) * 128:(t % 3) * 128 + 128],
                                       x[:, m, TOK0[t] if t < 8 else SEQ:(TOK0[t] if t < 8 else SEQ) + w], idn[:, :])
                ins.then_inc(y_t, 1)


_INS = ['x_prompt', 'x_sample', 'cache_swa_k', 'cache_swa_v', 'state_ffn_conv', 'mix_norm_g', 'sgu_w_in', 'sgu_ln_g',
        'sgu_ln_b', 'sgu_w_s', 'sgu_b_s', 'sgu_w_out', 'attn_w_qkv', 'attn_q_norm', 'attn_k_norm', 'attn_sinks',
        'attn_w_o', 'ffn_norm_g', 'ffn_w_up', 'ffn_conv_w', 'ffn_conv_b', 'ffn_w_down']
_OUTS = [(1, SEQ, D), (NB, NT, D), (1, NB, NT, SGU), (1, 1, 128, NKV, HD), (1, 1, 128, NKV, HD),
         (1, NB, 128, NKV, HD), (1, NB, 128, NKV, HD), (2, 1, 2, 2 * DFF), (2, NB, 2, 2 * DFF)]


def kernel(**inputs):
    import concourse.bacc as _bacc
    from concourse.bass_utils import run_bass_kernel_spmd as _run

    nc = _bacc.Bacc("TRN2", target_bir_lowering=False, num_devices=1)
    arrays, args = {}, []
    table, rotary = constants()
    for name, a in [(n, inputs[n]) for n in _INS] + [("table", table), ("rotary", rotary)]:
        a = np.ascontiguousarray(a)
        arrays[f"in_{name}"] = a
        args.append(nc.dram_tensor(f"in_{name}", a.shape, mybir.dt.from_np(a.dtype), kind="ExternalInput").ap())
    for i, shape in enumerate(_OUTS):
        args.append(nc.dram_tensor(f"out_{i}", shape, mybir.dt.float32, kind="ExternalOutput").ap())
    step_program(nc, *args)
    r = _run(nc, [arrays], core_ids=[0])
    return tuple(r.results[0][f"out_{i}"] for i in range(len(_OUTS)))
```

```python
import concourse.bass as bass
from concourse import mybir
from contextlib import ExitStack

import numpy as np

D = 1024
SEQ = 1024
NB, NT = 8, 8
SAMP = NB * NT
T = SEQ + SAMP
TT = 9
PAST_LEN = 4096
SGU = 2048
GROUPS = 8
DFF = 2816
FT = DFF // 128
FI = FT // 2
NH, NKV, HD = 16, 4, 64
QKV = (NH + 2 * NKV) * HD
EPS = 1e-6
KT = D // 128
CH = ((0, 384), (384, 384), (768, 320))
TOK0 = [128 * t for t in range(8)] + [T - 128]
AW = 2 + SEQ + NB * (2 + NT)
CW = AW - 2
STEP = 2 + NT

P_V = 0
P_U = P_V + 8
P_OUT = P_U + 8
P_F = [P_OUT + 8, 0]
P_QKV = P_F[0] + 3 * FI
P_WO = P_QKV + 6
P_F[1] = P_WO + 4
PAIRS = P_F[1] + 3 * FI

A_U, B_U = 1, 1
A_O, B_O = A_U + 16, B_U + 16
A_F, B_F = [A_O + 4, 0], [B_O + 4, 0]
A_WO, B_WO = A_F[0] + 66, B_F[0] + 66
A_F[1], B_F[1] = A_WO + 4, B_WO + 4
A_END, B_END = A_F[1] + 66, B_F[1] + 66

C_ID, C_CUR, C_CURT, C_PRVT, C_SEL, C_BLK, C_BLC, C_NEW, C_OLD, C_END = np.cumsum(
    [0, 128, 128, 128, 128, 128, 64, 128, 8, 128]).tolist()


def constants():
    c = np.zeros((128, C_END), np.float32)
    r = np.arange(128)
    c[:, C_ID:C_ID + 128] = r[:, None] == r[None, :]
    c[:, C_CUR:C_CUR + 128] = r[None, :] <= r[:, None]
    c[:, C_CURT:C_CURT + 128] = r[:, None] <= r[None, :]
    c[:, C_PRVT:C_PRVT + 128] = r[:, None] > r[None, :]
    q = np.arange(SAMP)
    c[:, C_SEL + 64:C_SEL + 128] = r[:, None] == (q % NT)[None, :]
    c[64:, C_BLK:C_BLK + 64] = (q // NT)[:, None] == (q // NT)[None, :]
    c[:64, C_BLC + 64:C_BLC + 128] = ((q // NT)[:, None] == (q // NT)[None, :]) & ((q % NT)[None, :] <= (q % NT)[:, None])
    c[:64, C_BLC:C_BLC + 64] = (q // NT)[:, None] == (q // NT)[None, :]
    c[:64, C_NEW:C_NEW + 8] = r[None, :8] <= (q % NT)[:, None]
    c[:64, C_OLD:C_OLD + 128] = r[None, :] > (q % NT)[:, None]
    inv = np.power(10000.0, -np.arange(0, HD, 2) / HD).astype(np.float32)
    pos = np.zeros((128, TT), np.float32)
    for t in range(TT):
        pos[:, t] = TOK0[t] + r
    pos[64:, 8] = PAST_LEN + q % NT
    ang = (pos[:, :, None] * inv[None, None, :]).astype(np.float32)
    ang = ang.astype(np.float64)
    rot = np.stack([np.cos(ang), np.sin(ang)], 1).astype(np.float32)
    return c, rot.reshape(128, 2 * TT * 32)


def step_program(nc, x_prompt, x_sample, cache_swa_k, cache_swa_v, state_ffn_conv, mix_norm_g, sgu_w_in, sgu_ln_g,
                 sgu_ln_b, sgu_w_s, sgu_b_s, sgu_w_out, attn_w_qkv, attn_q_norm, attn_k_norm, attn_sinks, attn_w_o,
                 ffn_norm_g, ffn_w_up, ffn_conv_w, ffn_conv_b, ffn_w_down, table, rotary,
                 y_prompt, y_sample, v_rows, k_prompt, v_prompt, k_sample, v_sample, conv_prompt, conv_sample):
    f32, f32r, i32 = mybir.dt.float32, mybir.dt.float32r, mybir.dt.int32
    ALU, ACT, AX = mybir.AluOpType, mybir.ActivationFunctionType, mybir.AxisListType
    mult, add, sub = ALU.mult, ALU.add, ALU.subtract

    with ExitStack() as ctx:
        ctx.enter_context(nc.allow_non_contiguous_dma(reason="small vectors"))

        def sb(name, shape, dt=f32, stack=ctx):
            return stack.enter_context(nc.sbuf_tensor(name, shape, dt))

        def sem(name):
            return ctx.enter_context(nc.semaphore(name))

        idn = sb("idn", [128, 128])
        ones = sb("ones", [128, 128])
        gains = sb("gains", [128, 32])
        cw = sb("cw", [128, 2, 2, 2, 2 * FT])
        eps = sb("eps", [128, 1])
        ss = sb("ss", [128, 16])
        rt = sb("rt", [128, 16])
        xm = sb("xm", [128, TT, 128])
        wraw = sb("wraw", [128, 2, 1024])
        wh = sb("wh", [128, 2, 1024], f32r)
        wl = sb("wl", [128, 2, 1024], f32r)
        with ExitStack() as s:
            x = sb("x", [128, KT, T], stack=s)
            hh = sb("hh", [128, KT, T], f32r, s)
            hl = sb("hl", [128, KT, T], f32r, s)
            v = sb("v", [128, 16, TT, 128], stack=s)
        with ExitStack() as s:
            tabs = sb("tabs", [128, C_END], stack=s)
            selr = sb("selr", [128, 128], f32r, s)
            sb("gap0", [128, 34816 // 4 - C_END - 128], stack=s)
            sb("gap1", [128, 2 * KT * T], stack=s)
            xin = sb("xin", [128, TT, D], stack=s)
            junk = sb("junk", [128, D], stack=s)
            vecs = sb("vecs", [128, 5, 128], stack=s)
            wsr = sb("wsr", [128, GROUPS, 128], stack=s)
        with ExitStack() as s:
            vnh = sb("vnh", [128, TT, 128], f32r, s)
            vnl = sb("vnl", [128, TT, 128], f32r, s)
            u = sb("u", [128, T], stack=s)
            wth = sb("wth", [128, GROUPS, 128], f32r, s)
            wtl = sb("wtl", [128, GROUPS, 128], f32r, s)
            wsh = sb("wsh", [128, GROUPS, 64], f32r, s)
            wsl = sb("wsl", [128, GROUPS, 64], f32r, s)
            bsb = sb("bsb", [128, GROUPS, 128], stack=s)
            lng = sb("lng", [128, 2, 128], stack=s)
            lnb = sb("lnb", [128, 2, 128], stack=s)
            bst = sb("bst", [128, TT, 8, 6], stack=s)
            mv = sb("mv", [128, TT, 2], stack=s)
        with ExitStack() as s:
            sb("gap2", [128, KT * T], stack=s)
            gh = sb("gh", [128, 16, T], f32r, s)
            with ExitStack() as s2:
                gt = sb("gt", [128, 16, T], stack=s2)
            with ExitStack() as s2:
                gl = sb("gl", [128, 16, T], f32r, s2)
                ssum = sb("ssum", [128, T], stack=s2)
                sqt = sb("sqt", [128, T // 2], stack=s2)
        with ExitStack() as s:
            sb("gap3", [128, 3 * KT * T], stack=s)
            fh = sb("fh", [128, 3, T], f32r, s)
            fl = sb("fl", [128, 3, T], f32r, s)
            a_sb = sb("a_sb", [128, 2, AW + 10], stack=s)
            cv = sb("cv", [128, AW], stack=s)
            with ExitStack() as s2:
                cg = sb("cg", [128, AW], stack=s2)
                sg = sb("sg", [128, AW], stack=s2)
            with ExitStack() as s2:
                fhx = sb("fhx", [128, 1, T], f32r, s2)
                sb("gap9", [128, AW - T], stack=s2)
                flx = sb("flx", [128, 1, T], f32r, s2)
            sb("gap10", [128, 2 * AW], stack=s)
            mt = sb("mt", [128, T], stack=s)
            rbc = sb("rbc", [128, T], stack=s)
            stc = sb("stc", [128, 4, 18], stack=s)
            sto = sb("sto", [18, 4, 128], stack=s)
            pst = sb("pst", [16, 4, 128], stack=s)
        with ExitStack() as s:
            sb("gap5", [128, KT * T], stack=s)
            with ExitStack() as s2:
                kT = sb("kT", [128, 2, NKV, 128], stack=s2)
                vb = sb("vb", [128, 2, NKV * HD], stack=s2)
                qTe = sb("qTe", [128, KT, 128], stack=s2)
                with ExitStack() as s3:
                    qr = sb("qr", [128, 20 * HD], stack=s3)
                    t1 = sb("t1", [128, 2, 20 * HD], stack=s3)
                    with ExitStack() as s4:
                        t0 = sb("t0", [128, 2, 20 * HD], stack=s4)
                    sm = sb("sm", [128, 2, 512], stack=s3)
                    pr = sb("pr", [128, 2, 512], stack=s3)
                    pc = sb("pc", [128, 2, 512], stack=s3)
                    pp = sb("pp", [128, 2, 512], stack=s3)
                    qTo = sb("qTo", [128, KT, 128], stack=s3)
                with ExitStack() as s3:
                    qm = sb("qm", [128, KT, NB * 72], stack=s3)
                    kcT = sb("kcT", [128, NB, NKV, 128], stack=s3)
                    ssc = sb("ssc", [64, 16, 128], stack=s3)
                    with ExitStack() as s4:
                        vc = sb("vc", [128, NB, NKV * HD], stack=s4)
                        kc = sb("kc", [128, NB, NKV * HD], stack=s4)
                    with ExitStack() as s4:
                        sb("gap7", [64, NB * NKV * HD], stack=s4)
                        pn = sb("pn", [64, 16, 128], stack=s4)
                with ExitStack() as s3:
                    pcT = sb("pcT", [128, 16, 64], stack=s3)
                    pnT = sb("pnT", [128, 16, 64], stack=s3)
            sb("gap6", [128, 2 * KT * T], stack=s)
            qkv = sb("qkv", [128, TT, QKV], stack=s)
            rot = sb("rot", [128, 2, TT, 32], stack=s)
            tb2 = sb("tb2", [128, C_END], stack=s)
            gqk = sb("gqk", [128, 2, HD], stack=s)
            nsk = sb("nsk", [128, NH], stack=s)
            pbias = sb("pbias", [128, 8], stack=s)
            hs = sb("hs", [128, TT, 20], stack=s)
            rq = sb("rq", [128, TT], stack=s)
            stt = sb("stt", [128, 64], stack=s)
            tmp = sb("tmp", [128, 1024], stack=s)
        with ExitStack() as s:
            sb("gap4", [128, KT * T], stack=s)
            yst = sb("yst", [128, 2, 8, 128], stack=s)
            ysp = sb("ysp", [64, KT, 128], stack=s)

        ps = ctx.enter_context(nc.psum_tensor("ps", [128, 8, 512], f32))
        BANK = (0, 3)
        STATS = (1, 2, 3)

        w_in = [sem("w_in0"), sem("w_in1")]
        w_hi, w_lo = sem("w_hi"), sem("w_lo")
        w_used = sem("w_used")
        free = [sem("free_a"), sem("free_b")]
        t_in, x_in = sem("t_in"), [sem(f"x_in{i}") for i in range(5)]
        vec_in, ws_in, bs_in = sem("vec_in"), sem("ws_in"), sem("bs_in")
        sq_st, rt_sq, rt_rc, xn = sem("sq_st"), sem("rt_sq"), sem("rt_rc"), sem("xn")
        ws_msk, vec_t, vec_ok = sem("ws_msk"), sem("vec_t"), sem("vec_ok")
        ws_t, wt_hi, wt_lo, ws8_t, ws8_ok, sel_ok = (sem(n) for n in ("ws_t", "wt_hi", "wt_lo", "ws8_t", "ws8_ok", "sel_ok"))
        ones_ok, eps_ok = sem("ones_ok"), sem("eps_ok")
        x_t, h_hi, h_lo = sem("x_t"), sem("h_hi"), sem("h_lo")
        zero = sem("zero")
        tm_full, tm_free = sem("tm_full"), sem("tm_free")
        bn, bna, ln_sq, ln_rc = sem("bn"), sem("bna"), sem("ln_sq"), sem("ln_rc")
        ln_in = [sem("ln_in0"), sem("ln_in1")]
        ln, vn_hi, vn_lo, v_out = sem("ln"), sem("vn_hi"), sem("vn_lo"), [sem("v_out0"), sem("v_out1")]
        mixed, gated = sem("mixed"), sem("gated")
        g_hi, g_lo, xm_in, xm_used = sem("g_hi"), sem("g_lo"), sem("xm_in"), sem("xm_used")
        x_sq, x_ss = sem("x_sq"), sem("x_ss")
        stat, rb_sq, rb_ok = sem("stat"), sem("rb_sq"), sem("rb_ok")
        halo, conv0, conv, silu, mtok, f_hi, f_lo = (sem(n) for n in ("halo", "conv0", "conv", "silu", "mtok", "f_hi", "f_lo"))
        down = sem("down")
        past_in, past_t, state_c, state_t, state_o, state_out = (
            sem(n) for n in ("past_in", "past_t", "state_c", "state_t", "state_o", "state_out"))
        a_in, rq_sq, rq_ok = sem("a_in"), sem("rq_sq"), sem("rq_ok")
        hs_ok, hs_sq, hs_rc, nsk_ok = sem("hs_ok"), sem("hs_sq"), sem("hs_rc"), sem("nsk_ok")
        zero_a, nrm, rope0, rope, qk_t, qk_c, v_c = sem("zero_a"), sem("nrm"), sem("rope0"), sem("rope"), sem("qk_t"), sem("qk_c"), sem("v_c")
        s_full, s_cp, s_mrg, s_nm = sem("s_full"), sem("s_cp"), sem("s_mrg"), sem("s_nm")
        p_exp, p_nrm, p_t, p_msk = sem("p_exp"), sem("p_nrm"), sem("p_t"), sem("p_msk")
        o_full, o_ok = sem("o_full"), sem("o_ok")
        kc_in, kv_in, kv_out, kc_t, kc_c, smp = sem("kc_in"), sem("kv_in"), sem("kv_out"), sem("kc_t"), sem("kc_c"), sem("smp")
        z_q, z_s, z_n, z_a, z_t, z_tc = (sem(n) for n in ("z_q", "z_s", "z_n", "z_a", "z_t", "z_tc"))
        hold_act, hold_dve, hold_pool = sem("hold_act"), sem("hold_dve"), sem("hold_pool")
        y_t, y_c, y_out, ys_out = sem("y_t"), sem("y_c"), [sem("y_out0"), sem("y_out1")], sem("ys_out")

        block = ctx.enter_context(nc.Block())

        def at(c, m=0, i=None):
            return c if i is None else i * m + c

        def load(eng, src, s, k, p, m=0, i=None):
            if i is not None or p > 0:
                eng.wait_ge(w_lo, at(2 * p + s - 1, 2 * m, i))
            eng.dma_start(wraw[:, s, :].rearrange("p (k n) -> p k n", k=k),
                          src.rearrange("(k p) n -> p k n", p=128)).then_inc(w_in[s], 16)

        def hi(act, s, p, m=0, i=None):
            act.wait_ge(w_in[s], at(16 * (p + 1), 16 * m, i))
            if i is not None or p > 0:
                act.wait_ge(w_used, at(2 * p + s - 1, 2 * m, i))
            act.activation(wh[:, s, :], wraw[:, s, :], ACT.Copy).then_inc(w_hi, 1)

        def lo(dve, s, p, m=0, i=None):
            dve.wait_ge(w_hi, at(2 * p + s + 1, 2 * m, i))
            dve.tensor_tensor(wl[:, s, :], wraw[:, s, :], wh[:, s, :].bitcast(f32), sub).then_inc(w_lo, 1)

        def chunks(area, width=None):
            b = BANK[area]
            return ps[:, b:b + 2, 0:384], ps[:, b + 2, 0:320]

        def cut(row):
            return row[:, 0:768].rearrange("p (c n) -> p c n", c=2), row[:, 768:T]

        PARTS = ((wh, 0), (wh, 1), (wl, 0))

        def rows(pe, area, s, k, col, mov, start, stop):
            for n, (w, part) in enumerate(PARTS):
                for c, (c0, cn) in enumerate(CH):
                    ins = pe.matmul(ps[:, BANK[area] + c, 0:cn], w[:, s, col:col + 128], mov[part][:, k, c0:c0 + cn],
                                    start=start and n == 0, stop=stop and n == 2, skip_group_check=True)
            return ins

        def by_pairs(eng, tile):
            tile(0)
            tile(1)
            with eng.Fori(0, 2) as i:
                tile(2, i)
                tile(3, i)
            tile(6)
            tile(7)

        def x_tile(m, i=None):
            return x[:, bass.ds(at(m, 2, i), 1), :].rearrange("p o n -> p (o n)")

        def square_slot(n, h):
            return sqt[:, :] if n == 0 else xm[:, :, :].rearrange("p t n -> p (t n)")[:, h * (T // 2):(h + 1) * (T // 2)]

        x_mov, g_mov = (hh, hl), (gh, gl)

        S_BANK = ((3, 4), (5, 6))
        Z_NEW, Z_HEADS = 2, 10
        GROUPS_A = 4 * 8

        def piece_at(c):
            n, g = c // 4, c % 4
            return (n + 2, g - 2) if g >= 2 else (n + 1, 2) if g == 0 else None

        def for_steps(eng, step):
            for c in range(4):
                step(c)
            with eng.Fori(0, 3) as i:
                for c in range(4, 12):
                    step(c, i)
            for c in range(28, GROUPS_A):
                step(c)

        def attention_loads(sp):
            def qkv_pair(c, p, m=0, i=None):
                for s in range(2):
                    load(sp, attn_w_qkv[0, 512 * s:512 * s + 512, bass.ds(at(256 * c, 256 * m, i), 256)], s, 4, p, m, i)
            qkv_pair(0, P_QKV)
            sp.wait_ge(w_used, 2 * P_QKV)
            sp.wait_ge(state_out, 32 * FI)
            sp.dma_start(rot[:, :, :, :].rearrange("p a t n -> p (a t n)"), rotary).then_inc(a_in, 16)
            sp.dma_start(tb2[:, :], table).then_inc(a_in, 16)
            sp.dma_start(gqk[:, 0, :], attn_q_norm[0].partition_broadcast(128)).then_inc(a_in, 16)
            sp.dma_start(gqk[:, 1, :], attn_k_norm[0].partition_broadcast(128)).then_inc(a_in, 16)
            sp.dma_start(nsk[:, :], attn_sinks[0].partition_broadcast(128)).then_inc(a_in, 16)
            with sp.Fori(0, 5) as i:
                qkv_pair(1, P_QKV + 1, 1, i)

            def wo_pair(c, p, m=0, i=None):
                for s in range(2):
                    load(sp, attn_w_o[0, :, bass.ds(at(256 * c + 128 * s, 256 * m, i), 128)], s, 8, p, m, i)
            wo_pair(0, P_WO)
            for src, dst in ((cache_swa_k, k_sample), (cache_swa_v, v_sample)):
                sp.dma_start(dst[0, :, 0:128 - NT].rearrange("b w h d -> b (w h d)"),
                             src[0, :, NT:128].rearrange("b w h d -> b (w h d)")).then_inc(kv_out, 16)
            sp.wait_ge(rope, ROPE * 7)
            sp.dma_start(k_prompt[0, 0].rearrange("w h d -> w (h d)"), qr[:, 1024:1280]).then_inc(kv_out, 16)
            sp.dma_start(v_prompt[0, 0].rearrange("w h d -> w (h d)"), qkv[:, 7, 1280:1536]).then_inc(kv_out, 16)
            sp.wait_ge(w_used, 2 * P_WO)
            sp.dma_start(kc[:, :, :], cache_swa_k[0].rearrange("b w h d -> w b (h d)")).then_inc(kc_in, 16)
            sp.wait_ge(rope, ROPE * 8)
            for b in range(NB):
                sp.dma_start(k_sample[0, b, 128 - NT:128].rearrange("w h d -> w (h d)"),
                             qr[64 + NT * b:64 + NT * b + NT, 1024:1280]).then_inc(smp, 16)
                sp.dma_start(v_sample[0, b, 128 - NT:128].rearrange("w h d -> w (h d)"),
                             qkv[64 + NT * b:64 + NT * b + NT, 8, 1280:1536]).then_inc(smp, 16)
            sp.wait_ge(o_ok, GROUPS_A)
            sp.dma_start(vc[:, :, :], cache_swa_v[0].rearrange("b w h d -> w b (h d)")).then_inc(kv_in, 16)
            with sp.Fori(0, 3) as i:
                wo_pair(1, P_WO + 1, 1, i)

        def attention_pool(pool):
            pool.wait_ge(w_used, 2 * P_WO)
            pool.memset(kT[:, 1, :, :], 0.0).then_inc(zero_a, 1)
            pool.memset(vb[:, 1, :], 0.0).then_inc(zero_a, 1)
            pool.memset(pbias[:, :], 0.0).then_inc(zero_a, 1)
            pool.wait_ge(zero_a, 3)
            pool.memset(pbias[:, 0:1], -1e30).then_inc(zero_a, 1)
            rotate(pool, t1, rope, 1)
            with pool.Fori(0, 6) as i:
                rotate(pool, t1, rope, 2, i)
            rotate(pool, t1, rope, 8)
            pool.wait_ge(qk_t, 27)
            pool.wait_ge(smp, 2 * NB * 16)
            pool.wait_ge(o_ok, GROUPS_A)
            pool.memset(qm[:, :, :], 0.0).then_inc(zero_a, 1)
            pool.wait_ge(kc_t, NB)
            pool.memset(pn[:, :, :], 0.0).then_inc(zero_a, 1)

        ROPE = 6

        def attention_act(act, squares):
            def qkv_block(b, m=0, i=None, values=False):
                hi(act, 0, P_QKV + 1 + b, m, i)
                for t in range(0, TT, 2):
                    bank = t // 2
                    if t < 8:
                        act.wait_ge(tm_full, at(32 + 4 * b + bank + 1, 4 * m, i))
                    else:
                        act.wait_ge(w_used, at(2 * (P_QKV + b) + 2, 2 * m, i))
                    if values:
                        pass
                    elif i is not None:
                        n = 5 * b + (0 if bank == 0 else -1 if bank == 1 else bank - 1)
                        act.wait_ge(hs_ok, at(n, 5 * m, i))
                    elif bank >= 2:
                        act.wait_ge(hs_ok, bank - 1)
                    for t_ in range(t, min(t + 2, TT)):
                        src = ps[:, bank, 256 * (t_ - t):256 * (t_ - t) + 256]
                        ins = act.activation(qkv[:, t_, bass.ds(at(256 * b, 256 * m, i), 256)], src, ACT.Copy,
                                             scale=rq[:, t_:t_ + 1])
                        if not values:
                            ins = act.activation(tmp[:, 512 * (bank % 2) + 256 * (t_ - t):512 * (bank % 2) + 256 * (t_ - t) + 256],
                                             src, ACT.Square, scale=rq[:, t_:t_ + 1])
                    ins.then_inc(tm_free, 1)
                hi(act, 1, P_QKV + 1 + b, m, i)

            act.wait_ge(stat, 2)
            act.activation(rq[:, :], ps[:, 6, 0:TT], ACT.Sqrt, scale=1.0 / D, bias=eps[:, :]).then_inc(rq_sq, 1)
            act.wait_ge(rq_ok, 1)
            act.wait_ge(state_out, 32 * FI)
            qkv_block(0)
            with act.Fori(0, 4) as i:
                qkv_block(1, 1, i)
            act.wait_ge(hs_ok, 25)
            act.activation(hs[:, :, :], hs[:, :, :], ACT.Sqrt, scale=1.0 / HD, bias=eps[:, :]).then_inc(hs_sq, 1)
            qkv_block(5, values=True)

            def take_piece(n, j, i=None):
                act.wait_ge(qk_t, at(3 * n + j + 1, 6, i))
                dst = (qTe, qTo)[n % 2][:, 4 * j:4 * j + 4, :] if j < 2 else kT[:, n % 2, :, :]
                act.activation(dst.rearrange("p k n -> p (k n)"), ps[:, 0, :], ACT.Copy).then_inc(qk_c, 1)

            def take_v(n, i=None):
                if n:
                    act.wait_ge(o_full, at(4 * n, 8, i))
                if i is not None:
                    act.sem_inc(hold_act, 1)
                act.activation(vb[:, n % 2, :], qkv[:, bass.ds(at(n, 2, i), 1), 1280:1536].rearrange("p o n -> p (o n)"),
                               ACT.Copy).then_inc(v_c, 1)

            def copy_prev(c, i=None):
                act.wait_ge(s_full, at(c + 1, 8, i))
                if c >= 2:
                    act.wait_ge(p_exp, at(c - 1, 8, i))
                b = S_BANK[c % 2][0]
                first = 0 if c < 4 and i is None else 1
                act.activation(sm[:, c % 2, :].rearrange("p (e n) -> p e n", e=2), ps[:, b:b + 2, 256:512], ACT.Identity,
                               bias=pbias[:, first:first + 1]).then_inc(s_cp, 1)

            def exps(c, i=None):
                z = c % 2
                act.wait_ge(s_nm, at(2 * c + 2, 16, i))
                if c >= 2:
                    act.wait_ge(p_t, at(c - 1, 8, i))
                for h in range(4):
                    act.activation(pr[:, z, 128 * h:128 * h + 128], sm[:, z, 128 * h:128 * h + 128], ACT.Exp,
                                   bias=stt[:, 8 * z + h:8 * z + h + 1], scale=HD ** -0.5,
                                   accum_out=stt[:, 16 + 8 * z + h:17 + 8 * z + h])
                act.activation(stt[:, 20 + 8 * z:24 + 8 * z], stt[:, 4 + 8 * z:8 + 8 * z], ACT.Exp).then_inc(p_exp, 1)

            def take_o(c, i=None):
                g = c % 4
                act.wait_ge(o_full, at(c + 1, 8, i))
                if i is not None:
                    act.sem_inc(hold_act, 1)
                act.activation(qkv[:, bass.ds(at(c // 4, 2, i), 1), 256 * g:256 * g + 256].rearrange("p o n -> p (o n)"),
                               ps[:, 1 + c % 2, 0:256], ACT.Copy).then_inc(o_ok, 1)

            def step(c, i=None):
                more = i is not None or c + 3 < GROUPS_A
                if more:
                    copy_prev(c + 3, i)
                piece = piece_at(c)
                if piece is not None and piece[0] <= 8:
                    take_piece(*piece, i)
                if c % 4 == 3:
                    take_v(c // 4 + 1, i)
                take_o(c, i)
                if more:
                    exps(c + 3, i)

            act.wait_ge(zero_a, 4)
            for j in range(3):
                take_piece(0, j)
            take_v(0)
            copy_prev(0)
            copy_prev(1)
            exps(0)
            copy_prev(2)
            take_piece(1, 0)
            take_piece(1, 1)
            exps(1)
            exps(2)
            for_steps(act, step)

            for b in range(0, NB):
                act.wait_ge(kc_t, b + 1)
                act.activation(kcT[:, b, :, :].rearrange("p g n -> p (g n)"), ps[:, 3 + b % 4, :], ACT.Copy).then_inc(kc_c, 1)
            for e in range(2):
                act.wait_ge(z_s, 2 + e)
                act.activation(ssc[:, 8 * e:8 * e + 8, :].rearrange("p (a h) n -> p a (h n)", a=2), ps[0:64, 3 + 2 * e:5 + 2 * e, :],
                               ACT.Copy).then_inc(z_a, 1)
                act.wait_ge(z_n, Z_NEW + Z_HEADS * e + 4)
                act.activation(ssc[:, 8 * e:8 * e + 8, :], ssc[:, 8 * e:8 * e + 8, :], ACT.Exp).then_inc(z_a, 1)
                act.activation(stt[0:64, 32 + 8 * e:40 + 8 * e], stt[0:64, 16 + 8 * e:24 + 8 * e], ACT.Exp).then_inc(z_a, 1)
            for e in range(2):
                act.wait_ge(z_t, e + 1)
                act.activation(pcT[:, 8 * e:8 * e + 8, :].rearrange("p h n -> p (h n)"), ps[:, 3 + 2 * e, :], ACT.Copy)
                act.activation(pnT[:, 8 * e:8 * e + 8, :].rearrange("p h n -> p (h n)"), ps[:, 4 + 2 * e, :], ACT.Copy).then_inc(z_tc, 1)
            act.wait_ge(z_t, 3)
            act.activation(qkv[:, 8, 0:1024].rearrange("p (k n) -> p k n", k=KT)[:, :, 0:64],
                           ps[:, 2, :].rearrange("p (k n) -> p k n", k=KT), ACT.Copy).then_inc(o_ok, 1)

            act.wait_ge(o_ok, GROUPS_A + 1)
            for k in range(KT):
                act.activation(hh[:, k, 0:SEQ].rearrange("p (t n) -> p t n", n=128), qkv[:, 0:8, 128 * k:128 * k + 128], ACT.Copy)
                act.activation(hh[:, k, SEQ:T], qkv[:, 8, 128 * k:128 * k + 64], ACT.Copy).then_inc(h_hi, 1)

            def wo_tile(m, i=None):
                if m == 7:
                    return
                act.wait_ge(w_used, at(2 * P_WO + m + 1, 2, i))
                hi(act, m % 2, P_WO + 1 + m // 2, 1, i)
                act.wait_ge(free[m % 2], at((A_WO, B_WO)[m % 2] + m // 2 + 1, 1, i))
                squares(2, m, i)

            by_pairs(act, wo_tile)

        def rotate(eng, t, turned, n, i=None):
            ti = bass.ds(at(n, 1, i), 1)
            r0 = ROPE * max(n - 1, 0)

            def after(semaphore, k, m):
                eng.wait_ge(semaphore, at(k, m, i))
                if i is not None:
                    eng.sem_inc(hold_pool, 1)

            def halves(a):
                return a.rearrange("p (h c d) -> p h c d", c=2, d=32)

            if n >= 2:
                after(turned, r0, ROPE)
            after(nrm, 2 * n + 2, 2)
            src = halves(qkv[:, ti, 0:1280].rearrange("p o n -> p (o n)"))
            cos = rot[:, 0, ti, :].rearrange("p o n -> p (o n)").unsqueeze(1).to_broadcast([128, 20, 32])
            sin = rot[:, 1, ti, :].rearrange("p o n -> p (o n)").unsqueeze(1).to_broadcast([128, 20, 32])
            for c in range(2):
                eng.tensor_tensor(halves(t[:, 0, :])[:, :, c, :], src[:, :, c, :], cos, mult).then_inc(turned, 1)
                eng.tensor_tensor(halves(t[:, 1, :])[:, :, c, :], src[:, :, 1 - c, :], sin, mult).then_inc(turned, 1)
            after(turned, r0 + 4, ROPE)
            if n:
                after(qk_t, 3 * n, 3)
            if n == 8:
                eng.wait_ge(kv_out, 16 * 4)
            for c, op in ((0, sub), (1, add)):
                eng.tensor_tensor(halves(qr[:, :])[:, :, c, :], halves(t[:, 0, :])[:, :, c, :], halves(t[:, 1, :])[:, :, c, :],
                                  op).then_inc(turned, 1)

        def attention_dve(dve):
            dve.wait_ge(rq_sq, 1)
            dve.reciprocal(rq[:, :], rq[:, :]).then_inc(rq_ok, 1)
            dve.wait_ge(a_in, 80)
            dve.tensor_scalar(nsk[:, :], nsk[:, :], -1.0, None, mult).then_inc(nsk_ok, 1)

            def sums(b, m=0, i=None):
                lo(dve, 0, P_QKV + 1 + b, m, i)
                for t in range(0, TT, 2):
                    bank, tn = t // 2, min(2, TT - t)
                    dve.wait_ge(tm_free, at(40 + 5 * b + bank + 1, 5 * m, i))
                    dve.tensor_reduce(hs[:, t:t + tn, bass.ds(at(4 * b, 4 * m, i), 4)],
                                      tmp[:, 512 * (bank % 2):512 * (bank % 2) + 256 * tn].rearrange("p (t h d) -> p t h d", h=4, d=HD),
                                      AX.X, add).then_inc(hs_ok, 1)
                lo(dve, 1, P_QKV + 1 + b, m, i)
            sums(0)
            with dve.Fori(0, 4) as i:
                sums(1, 1, i)
            dve.wait_ge(hs_sq, 1)
            dve.reciprocal(hs[:, :, :], hs[:, :, :]).then_inc(hs_rc, 1)

            def head_norm(t):
                row = qkv[:, t, 0:1280].rearrange("p (h d) -> p h d", d=HD)
                dve.tensor_tensor(row, row, hs[:, t, :].unsqueeze(2).to_broadcast([128, 20, HD]), mult).then_inc(nrm, 1)
                dve.wait_ge(nrm, 2 * t + 1)
                dve.tensor_tensor(row[:, 0:16], row[:, 0:16], gqk[:, 0, :].unsqueeze(1).to_broadcast([128, 16, HD]), mult)
                dve.tensor_tensor(row[:, 16:20], row[:, 16:20], gqk[:, 1, :].unsqueeze(1).to_broadcast([128, 4, HD]),
                                  mult).then_inc(nrm, 1)

            dve.wait_ge(hs_rc, 1)
            for t in range(6):
                head_norm(t)
            for s in range(2):
                lo(dve, s, P_WO)

            def merge(c, i=None):
                g, z = c % 4, c % 2
                b = S_BANK[z][0]
                dve.wait_ge(s_cp, at(c + 1, 8, i))
                if i is not None:
                    dve.sem_inc(hold_dve, 1)
                sv = sm[:, z, :].rearrange("p (e j n) -> p e j n", e=2, j=2)
                for e in range(2):
                    ins = dve.copy_predicated(sv[:, e], tb2[:, C_CUR:C_CUR + 128].bitcast(i32).unsqueeze(1).to_broadcast([128, 2, 128]),
                                              ps[:, b + e, 0:256].rearrange("p (j n) -> p j n", j=2))
                ins.then_inc(s_mrg, 1)
                dve.wait_ge(s_mrg, at(2 * c + 1, 16, i))
                dve.reduce_max(stt[:, 48 + 4 * z:52 + 4 * z], sm[:, z, :].rearrange("p (h n) -> p h n", h=4), AX.X).then_inc(s_mrg, 1)
                dve.wait_ge(s_mrg, at(2 * c + 2, 16, i))
                ns = nsk[:, 4 * g:4 * g + 4].rearrange("p (j e) -> p e j", e=2)
                nm = stt[:, 8 * z:8 * z + 4].rearrange("p (e j) -> p e j", e=2)
                dve.scalar_tensor_tensor(nm, stt[:, 48 + 4 * z:52 + 4 * z].rearrange("p (e j) -> p e j", e=2), -HD ** -0.5, ns,
                                         mult, ALU.min).then_inc(s_nm, 1)
                dve.wait_ge(s_nm, at(2 * c + 1, 16, i))
                dve.tensor_tensor(stt[:, 4 + 8 * z:8 + 8 * z].rearrange("p (e j) -> p e j", e=2), nm, ns, sub).then_inc(s_nm, 1)

            def normalise(c, i=None):
                z = c % 2
                dve.wait_ge(p_exp, at(c + 1, 8, i))
                dn = stt[:, 16 + 8 * z:20 + 8 * z]
                dve.tensor_tensor(dn, dn, stt[:, 20 + 8 * z:24 + 8 * z], add).then_inc(p_nrm, 1)
                dve.wait_ge(p_nrm, at(3 * c + 1, 24, i))
                dve.reciprocal(dn, dn).then_inc(p_nrm, 1)
                dve.wait_ge(p_nrm, at(3 * c + 2, 24, i))
                pv = pr[:, z, :].rearrange("p (h n) -> p h n", h=4)
                dve.tensor_tensor(pv, pv, dn.unsqueeze(2).to_broadcast([128, 4, 128]), mult).then_inc(p_nrm, 1)

            def mask(c, i=None):
                z = c % 2
                dve.wait_ge(p_t, at(c + 1, 8, i))
                if c >= 2:
                    dve.wait_ge(o_full, at(c - 1, 8, i))
                for dst, col in ((pc, C_CURT), (pp, C_PRVT)):
                    ins = dve.tensor_tensor(dst[:, z, :].rearrange("p (h n) -> p h n", h=4), ps[:, 7, :].rearrange("p (h n) -> p h n", h=4),
                                            tb2[:, col:col + 128].unsqueeze(1).to_broadcast([128, 4, 128]), mult)
                ins.then_inc(p_msk, 1)

            def step(c, i=None):
                mask(c, i)
                if i is not None or c + 1 < GROUPS_A:
                    normalise(c + 1, i)
                if i is not None or c + 3 < GROUPS_A:
                    merge(c + 3, i)

            dve.wait_ge(nsk_ok, 1)
            dve.wait_ge(w_used, 2 * P_WO)
            rotate(dve, t0, rope0, 0)
            for t in range(6, TT):
                head_norm(t)
            merge(0)
            merge(1)
            normalise(0)
            merge(2)
            for_steps(dve, step)

            dve.wait_ge(zero_a, 5)
            dve.wait_ge(qk_c, 27)
            dve.tensor_copy(qm[:, :, :].rearrange("p k (b n) -> p k b n", n=72)[:, :, :, 0:NT],
                            qTe[:, :, 64:128].rearrange("p k (b n) -> p k b n", n=NT)).then_inc(z_q, 1)
            dve.wait_ge(z_s, 1)
            tv = tmp[0:64, :]
            dve.tensor_tensor(tv.rearrange("p (a h n) -> p a h n", a=2, n=64), ps[0:64, 0:2, :].rearrange("p a (h n) -> p a h n", n=64),
                              tb2[0:64, C_BLC:C_BLC + 64].unsqueeze(1).unsqueeze(1).to_broadcast([64, 2, 8, 64]), mult).then_inc(z_n, 1)
            dve.wait_ge(z_n, 1)
            new = hs[0:64, :, :].rearrange("p t h -> p (t h)")[:, 0:128].rearrange("p (h n) -> p h n", h=16)
            dve.tensor_reduce(new, tv.rearrange("p (h b n) -> p h n b", h=16, b=NB), AX.X, add).then_inc(z_n, 1)
            dve.wait_ge(z_n, 2)
            dve.wait_ge(zero_a, 6)
            for e in range(2):
                z = Z_NEW + Z_HEADS * e
                sc = ssc[:, 8 * e:8 * e + 8, :]
                dve.wait_ge(z_a, 3 * e + 1)
                dve.copy_predicated(sc[:, :, 0:NT], tb2[0:64, C_NEW:C_NEW + NT].bitcast(i32).unsqueeze(1).to_broadcast([64, 8, NT]),
                                    new[:, 8 * e:8 * e + 8, :]).then_inc(z_n, 1)
                dve.wait_ge(z_n, z + 1)
                dve.reduce_max(stt[0:64, 48 + 8 * e:56 + 8 * e], sc, AX.X).then_inc(z_n, 1)
                dve.wait_ge(z_n, z + 2)
                mx = stt[0:64, 48 + 8 * e:56 + 8 * e].rearrange("p (g j) -> p g j", j=2)
                nm = stt[0:64, 8 * e:8 * e + 8].rearrange("p (g j) -> p g j", j=2)
                sk = stt[0:64, 16 + 8 * e:24 + 8 * e].rearrange("p (g j) -> p g j", j=2)
                ns = nsk[0:64, :].rearrange("p (g j e) -> p e g j", e=2, j=2)[:, e]
                dve.scalar_tensor_tensor(nm, mx, -HD ** -0.5, ns, mult, ALU.min).then_inc(z_n, 1)
                dve.wait_ge(z_n, z + 3)
                dve.tensor_tensor(sk, nm, ns, sub)
                dve.scalar_tensor_tensor(sc, sc, HD ** -0.5, stt[0:64, 8 * e:8 * e + 8].unsqueeze(2).to_broadcast([64, 8, 128]),
                                         mult, add).then_inc(z_n, 1)
                dve.wait_ge(z_a, 3 * e + 3)
                dn = stt[0:64, 48 + 8 * e:56 + 8 * e]
                dve.tensor_reduce(dn, sc, AX.X, add).then_inc(z_n, 1)
                dve.wait_ge(z_n, z + 5)
                dve.tensor_tensor(dn, dn, stt[0:64, 32 + 8 * e:40 + 8 * e], add).then_inc(z_n, 1)
                dve.wait_ge(z_n, z + 6)
                dve.reciprocal(dn, dn).then_inc(z_n, 1)
                dve.wait_ge(z_n, z + 7)
                dve.tensor_tensor(sc, sc, dn.unsqueeze(2).to_broadcast([64, 8, 128]), mult).then_inc(z_n, 1)
                dve.wait_ge(z_n, z + 8)
                dve.tensor_tensor(pn[:, 8 * e:8 * e + 8, 64:128].rearrange("p h (b n) -> p h b n", n=NT),
                                  sc[:, :, 0:NT].unsqueeze(2).to_broadcast([64, 8, NB, NT]),
                                  tb2[0:64, C_BLC + 64:C_BLC + 128].rearrange("p (b n) -> p b n", n=NT).unsqueeze(1).to_broadcast([64, 8, NB, NT]),
                                  mult).then_inc(z_n, 1)
                dve.wait_ge(z_n, z + 9)
                dve.tensor_tensor(sc[:, :, 0:NT], sc[:, :, 0:NT], tb2[0:64, C_OLD:C_OLD + NT].unsqueeze(1).to_broadcast([64, 8, NT]),
                                  mult).then_inc(z_n, 1)

            for k in range(KT):
                dve.wait_ge(h_hi, 24 + k + 1)
                dve.tensor_tensor(hl[:, k, 0:SEQ].rearrange("p (t n) -> p t n", n=128), qkv[:, 0:8, 128 * k:128 * k + 128],
                                  hh[:, k, 0:SEQ].bitcast(f32).rearrange("p (t n) -> p t n", n=128), sub)
                dve.tensor_tensor(hl[:, k, SEQ:T], qkv[:, 8, 128 * k:128 * k + 64], hh[:, k, SEQ:T].bitcast(f32), sub).then_inc(h_lo, 1)

            def wo_tile(m, i=None):
                if m == 7:
                    return
                area = m % 2
                dve.wait_ge(w_used, at(2 * P_WO + m + 1, 2, i))
                if i is not None:
                    dve.sem_inc(hold_dve, 1)
                for dst, src in zip(cut(x_tile(m, i)), chunks(area)):
                    ins = dve.tensor_tensor(dst, dst, src, add)
                ins.then_inc(free[area], 1)
                lo(dve, m % 2, P_WO + 1 + m // 2, 1, i)

            by_pairs(dve, wo_tile)

        def keys_twice(pe, bank, keys):
            for g in range(NKV - 1):
                pe.transpose(ps[:, bank, 128 * g:128 * g + 128], keys[:, HD * g:HD * g + 2 * HD], idn[:, :])
            for e, g in ((0, NKV - 1), (1, 0)):
                ins = pe.matmul(ps[64 * e:64 * e + 64, bank, 384:512], keys[:, HD * g:HD * g + HD], idn[:, :], start=True, stop=True)
            return ins

        def attention_pe(pe, token_major):
            for a in (0, 1):
                pe.wait_ge(free[a], (A_WO, B_WO)[a])
            pe.wait_ge(halo, 4 * FI)
            token_major(P_QKV, None, first=16)
            pe.wait_ge(x_ss, 32)
            for t in range(TT):
                ins = pe.matmul(ps[:, 6, t:t + 1], ssum[:, TOK0[t]:TOK0[t] + 128], ones[:, 0:1], start=True, stop=True)
            ins.then_inc(stat, 1)
            with pe.Fori(0, 5) as i:
                token_major(P_QKV + 1, 8, 1, i)
            pe.wait_ge(tm_free, 70)
            pe.wait_ge(zero_a, 2)

            def transposes(n, j, i=None):
                if j == 0:
                    if n:
                        pe.wait_ge(rope, at(ROPE * n, 2 * ROPE, i))
                    else:
                        pe.wait_ge(rope0, ROPE)
                if n or j:
                    pe.wait_ge(qk_c, at(3 * n + j, 6, i))
                if j < 2:
                    for k in range(4):
                        ins = pe.transpose(ps[:, 0, k * 128:k * 128 + 128], qr[:, 128 * (4 * j + k):128 * (4 * j + k) + 128], idn[:, :])
                else:
                    ins = keys_twice(pe, 0, qr[:, 1024:1280])
                ins.then_inc(qk_t, 1)

            def scores(c, i=None):
                n, g = c // 4, c % 4
                qT = (qTe, qTo)[n % 2]
                if g == 0:
                    pe.wait_ge(qk_c, at(3 * n + 3, 6, i))
                if c >= 2:
                    pe.wait_ge(s_mrg, at(2 * (c - 2) + 1, 16, i))
                for old in range(2):
                    for j in range(2):
                        for e in range(2):
                            ins = pe.matmul(ps[:, S_BANK[c % 2][e], 256 * old + 128 * j:256 * old + 128 * j + 128],
                                            qT[64 * e:64 * e + 64, 2 * g + j, :],
                                            kT[64 * e:64 * e + 64, (n + old) % 2, (g - e) % NKV, :], start=True, stop=True)
                ins.then_inc(s_full, 1)

            def probs(c, i=None):
                pe.wait_ge(p_nrm, at(3 * c + 3, 24, i))
                if c:
                    pe.wait_ge(p_msk, at(c, 8, i))
                for h in range(4):
                    ins = pe.transpose(ps[:, 7, 128 * h:128 * h + 128], pr[:, c % 2, 128 * h:128 * h + 128], idn[:, :])
                ins.then_inc(p_t, 1)

            def output(c, i=None):
                n, g = c // 4, c % 4
                if g == 0:
                    pe.wait_ge(v_c, at(n + 1, 2, i))
                pe.wait_ge(p_msk, at(c + 1, 8, i))
                if c >= 2:
                    pe.wait_ge(o_ok, at(c - 1, 8, i))
                for e in range(2):
                    for old, src in ((0, pc), (1, pp)):
                        ins = pe.matmul(ps[64 * e:64 * e + 64, 1 + c % 2, 0:256], vb[:, (n + old) % 2, HD * g:HD * g + HD],
                                        src[:, c % 2, 256 * e:256 * e + 256], start=old == 0, stop=old == 1)
                ins.then_inc(o_full, 1)

            def step(c, i=None):
                probs(c, i)
                if i is not None or c + 3 < GROUPS_A:
                    scores(c + 3, i)
                piece = piece_at(c)
                if piece is not None and piece[0] <= 8:
                    transposes(*piece, i)
                output(c, i)

            for j in range(3):
                transposes(0, j)
            scores(0)
            scores(1)
            scores(2)
            transposes(1, 0)
            transposes(1, 1)
            for_steps(pe, step)

            pe.wait_ge(kc_in, 16)
            for b in range(NB):
                if b >= 4:
                    pe.wait_ge(kc_c, b - 3)
                keys_twice(pe, 3 + b % 4, kc[:, b, :]).then_inc(kc_t, 1)
            pe.wait_ge(o_ok, GROUPS_A)
            for e in range(2):
                for g in range(NKV):
                    for j in range(2):
                        ins = pe.matmul(ps[0:64, e, 128 * g + 64 * j:128 * g + 64 * j + 64], qTe[64 * e:64 * e + 64, 2 * g + j, 64:128],
                                        kT[64 * e:64 * e + 64, 0, (g - e) % NKV, 64:128], start=True, stop=True)
            ins.then_inc(z_s, 1)
            pe.wait_ge(kc_c, NB)
            pe.wait_ge(z_q, 1)
            for e in range(2):
                for g in range(NKV):
                    for j in range(2):
                        o = ps[0:64, 3 + 2 * e + g // 2, 256 * (g % 2) + 128 * j:256 * (g % 2) + 128 * j + 128]
                        for b in range(NB):
                            ins = pe.matmul(o, qm[64 * e:64 * e + 64, 2 * g + j, 64 * b:64 * b + 64],
                                            kcT[64 * e:64 * e + 64, b, (g - e) % NKV, :], start=b == 0, stop=b == NB - 1)
                ins.then_inc(z_s, 1)
            pe.wait_ge(kv_in, 16)
            for e in range(2):
                pe.wait_ge(z_n, Z_NEW + Z_HEADS * (e + 1))
                for src, bank in ((ssc, 3 + 2 * e), (pn, 4 + 2 * e)):
                    for h in range(8):
                        ins = pe.transpose(ps[:, bank, 64 * h:64 * h + 64], src[:, 8 * e + h, :], idn[0:64, 0:64])
                ins.then_inc(z_t, 1)
            for e in range(2):
                pe.wait_ge(z_tc, e + 1)
                for g in range(NKV):
                    h = 8 * e + 2 * g
                    o = ps[64 * e:64 * e + 64, 2, 128 * g:128 * g + 128].rearrange("p (j n) -> p j n", j=2)
                    pe.matmul(o, vb[:, 0, HD * g:HD * g + HD], pnT[:, h:h + 2, :], start=True, stop=False, skip_group_check=True)
                    for b in range(NB):
                        ins = pe.matmul(o[:, :, NT * b:NT * b + NT], vc[:, b, HD * g:HD * g + HD], pcT[:, h:h + 2, NT * b:NT * b + NT],
                                        start=False, stop=True, skip_group_check=True)
            ins.then_inc(z_t, 1)

        def attention_out_pe(pe):
            pe.wait_ge(o_ok, GROUPS_A + 1)

            def wo_tile(m, i=None):
                area = m % 2
                pe.wait_ge(free[area], at((A_WO, B_WO)[area] + m // 2, 1, i))
                pe.wait_ge(w_lo, at(2 * P_WO + m + 1, 2, i))
                for k in range(KT):
                    if m == 0:
                        pe.wait_ge(h_lo, 24 + k + 1)
                    ins = rows(pe, area, m % 2, k, 128 * k, x_mov, k == 0, k == 7)
                ins.then_inc(w_used, 1)

            by_pairs(pe, wo_tile)

        @block.sync
        def _(sp):
            xv = x_prompt[0].rearrange("(t p) n -> p t n", p=128)
            for i in range(4):
                sp.dma_start(xin[:, 2 * i:2 * i + 2, :], xv[:, 2 * i:2 * i + 2, :]).then_inc(x_in[i], 16)
            sp.dma_start(xin[0:64, 8, :], x_sample.rearrange("b t n -> (b t) n")).then_inc(x_in[4], 16)
            sp.dma_start(idn[:, :], table[:, C_ID:C_ID + 128]).then_inc(t_in, 16)
            sp.dma_start(tabs[:, :], table).then_inc(t_in, 16)
            sp.dma_start(vecs[0:16, 0, :], mix_norm_g.rearrange("l (k p) -> (l k) p", p=128)).then_inc(vec_in, 16)
            sp.dma_start(vecs[16:32, 0, :], ffn_norm_g.rearrange("l (k p) -> (l k) p", p=128)).then_inc(vec_in, 16)
            for L in range(2):
                for j in range(2):
                    sp.dma_start(vecs[44 * j:44 * j + 44, 1 + 2 * L, :],
                                 ffn_conv_w[L, j].rearrange("(k p) -> k p", p=128)).then_inc(vec_in, 16)
                sp.dma_start(vecs[0:44, 2 + 2 * L, :],
                             ffn_conv_w[L, 2].rearrange("(k p) -> k p", p=128)).then_inc(vec_in, 16)
                sp.dma_start(vecs[44:88, 2 + 2 * L, :],
                             ffn_conv_b[L].rearrange("(k p) -> k p", p=128)).then_inc(vec_in, 16)
            sp.dma_start(wsr[:, :, :], sgu_w_s[0].rearrange("g t s -> t g s")).then_inc(ws_in, 16)

            def v_pair(m=0, i=None):
                for s in range(2):
                    load(sp, sgu_w_in[0, 512 * s:512 * s + 512, bass.ds(at(SGU, 256 * m, i), 256)], s, 4, P_V, m, i)

            v_pair()
            with sp.Fori(1, 8) as i:
                v_pair(1, i)

            sp.wait_ge(ws8_ok, 2)
            sp.dma_start(bsb[:, :, :].rearrange("p g n -> p (g n)"),
                         sgu_b_s[0].rearrange("g n -> (g n)").partition_broadcast(128)).then_inc(bs_in, 16)

            def u_unit(s, c, p, m=0, i=None):
                load(sp, sgu_w_in[0, :, bass.ds(at(128 * c, 256 * m, i), 128)], s, 8, p, m, i)

            def ln_gains(s, c, m=0, i=None):
                col = bass.ds(at(128 * c, 256 * m, i), 128)
                sp.dma_start(lng[:, s, :], sgu_ln_g[0, col].partition_broadcast(128)).then_inc(ln_in[s], 16)
                sp.dma_start(lnb[:, s, :], sgu_ln_b[0, col].partition_broadcast(128)).then_inc(ln_in[s], 16)

            for s in range(2):
                u_unit(s, s, P_U)
                ln_gains(s, s)
            with sp.Fori(0, 7) as i:
                for s in range(2):
                    u_unit(s, 2 + s, P_U + 1, 1, i)
                    sp.wait_ge(ln, at(3 * s + 3, 6, i))
                    ln_gains(s, 2 + s, 1, i)

            def xm_load(m, i=None, c=0):
                col = bass.ds(at(128 * c, 128, i), 128)
                sp.dma_start(xm[:, 0:8, :], xv[:, :, col]).then_inc(xm_in, 16)
                sp.dma_start(xm[0:64, 8, :], x_sample.rearrange("b t n -> (b t) n")[:, col]).then_inc(xm_in, 16)

            def out_pair(c, p, m=0, i=None):
                for s in range(2):
                    load(sp, sgu_w_out[0, 1024 * s:1024 * s + 1024, bass.ds(at(128 * c, 128 * m, i), 128)],
                         s, 8, p, m, i)

            out_pair(0, P_OUT)
            xm_load(0)
            with sp.Fori(0, 7) as i:
                out_pair(1, P_OUT + 1, 1, i)
                sp.wait_ge(xm_used, at(1, 1, i))
                xm_load(1, i, 1)

            def ffn_loads(L):
                P = P_F[L]

                def up_pair(q, c, p, m=0, i=None):
                    for s in range(2):
                        load(sp, ffn_w_up[L, :, bass.ds(at(DFF * s + 128 * (2 * c + q), 256, i), 128)], s, 8, p, m, i)

                def down_pair(c, p, m=0, i=None):
                    for s in range(2):
                        load(sp, ffn_w_down[L, bass.ds(at(256 * c, 256, i), 256), 512 * s:512 * s + 512],
                             s, 2, p, m, i)

                def past(c, i=None):
                    if i is not None or L or c:
                        sp.wait_ge(past_t, at(FI * L + c, 1, i))
                    src = state_ffn_conv[L].rearrange("b r (z n) -> (b r) z n", z=2)
                    sp.dma_start(pst[:, :, :].rearrange("p (z q) n -> p z (q n)", z=2),
                                 src[:, :, bass.ds(at(256 * c, 256, i), 256)]).then_inc(past_in, 16)

                up_pair(0, 0, P)
                up_pair(1, 0, P + 1)
                past(0)
                with sp.Fori(0, FI - 2) as i:
                    up_pair(0, 1, P + 2, 3, i)
                    past(1, i)
                    down_pair(0, P + 3, 3, i)
                    up_pair(1, 1, P + 4, 3, i)
                up_pair(0, FI - 1, P + 3 * FI - 4)
                past(FI - 1)
                up_pair(1, FI - 1, P + 3 * FI - 3)
                down_pair(FI - 2, P + 3 * FI - 2)
                down_pair(FI - 1, P + 3 * FI - 1)

            ffn_loads(0)
            attention_loads(sp)
            ffn_loads(1)
            for e in y_out:
                sp.wait_ge(e, 4 * 16)
            sp.wait_ge(ys_out, 16)
            for e in v_out:
                sp.wait_ge(e, 8 * 16)
            sp.wait_ge(kv_out, 4 * 16)
            sp.wait_ge(smp, 2 * NB * 16)
            sp.wait_ge(state_out, 2 * 32 * FI)

        @block.gpsimd
        def _(pool):
            pool.memset(ones[:, :], 1.0).then_inc(ones_ok, 1)

            def sum_squares(n):
                def tile(m, i=None):
                    for h in range(2):
                        half = ssum[:, h * (T // 2):(h + 1) * (T // 2)]
                        c = 16 * n + 2 * m + h
                        pool.wait_ge(x_sq, at(c + 1, 2, i))
                        if m == 0:
                            if n:
                                pool.wait_ge(stat, STATS[n - 1])
                            pool.tensor_copy(half, square_slot(n, h)).then_inc(x_ss, 1)
                        else:
                            pool.wait_ge(x_ss, at(c - 1, 2, i))
                            pool.tensor_tensor(half, half, square_slot(n, h), add).then_inc(x_ss, 1)
                tile(0)
                with pool.Fori(0, 7) as i:
                    tile(1, i)

            def zero_halos(L):
                pool.memset(a_sb[:, :, 0:2], 0.0).then_inc(zero, 1)

            sum_squares(0)
            zero_halos(0)
            sum_squares(1)
            attention_pool(pool)
            sum_squares(2)
            pool.wait_ge(h_lo, 40)
            zero_halos(1)

        @block.scalar
        def _(act):
            act.wait_ge(eps_ok, 1)
            act.activation(rt[:, 15:16], eps[:, :], ACT.Sqrt)
            for t in range(TT):
                n = 128 if t < 8 else 64
                if t % 2 == 0:
                    act.wait_ge(x_in[t // 2], 16)
                if t:
                    act.wait_ge(sq_st, t)
                act.activation(junk[0:n, :], xin[0:n, t, :], ACT.Square, accum_out=ss[0:n, t:t + 1]).then_inc(sq_st, 1)
                if t % 2 or t == 8:
                    a = t - 1 if t % 2 else t
                    act.wait_ge(sq_st, t + 1)
                    act.activation(rt[0:n, a:t + 1], ss[0:n, a:t + 1], ACT.Sqrt, scale=1.0 / D, bias=eps[0:n, :]).then_inc(rt_sq, 1)
            act.wait_ge(vec_t, 1)
            act.activation(gains[:, :], ps[:, 6, 0:32], ACT.Copy).then_inc(vec_ok, 1)
            act.activation(cw[:, :, :, :, :].rearrange("p l t r k -> p (l t r k)"), ps[:, 6, 32:384], ACT.Copy).then_inc(vec_ok, 1)
            act.wait_ge(t_in, 32)
            act.activation(selr[:, :], tabs[:, C_SEL:C_SEL + 128], ACT.Copy).then_inc(sel_ok, 1)
            for s in range(2):
                hi(act, s, P_V)
            act.wait_ge(vec_ok, 1)
            for k in range(KT):
                area = k % 2
                act.wait_ge(x_t, k + 1)
                for dst, src in zip(cut(hh[:, k, :]), chunks(area)):
                    ins = act.activation(dst, src, ACT.Identity, scale=gains[:, k:k + 1])
                ins.then_inc(h_hi, 1)
                if k == 0:
                    act.wait_ge(ws_t, 1)
                    act.activation(wth[:, :, :].rearrange("p (a g) n -> p a (g n)", a=2), ps[:, 3:5, :], ACT.Copy).then_inc(wt_hi, 1)

            def v_block(b, m=0, i=None):
                hi(act, 0, P_V + 1 + b, m, i)
                for t in range(0, TT, 2):
                    if t < 8:
                        act.wait_ge(tm_full, at(4 * b + t // 2 + 1, 4 * m, i))
                    else:
                        act.wait_ge(w_used, at(2 * (P_V + b) + 2, 2 * m, i))
                    tn = 2 if t < 8 else 1
                    for a in range(2):
                        src = ps[:, t // 2, 0:256 * tn].rearrange("p (t a n) -> p a t n", a=2, n=128)[:, a]
                        dst = v[:, bass.ds(at(2 * b + a, 2 * m, i), 1), t:t + tn, :].rearrange("p o t n -> p (o t) n")
                        ins = act.activation(dst, src, ACT.Gelu_apprx_tanh)
                    ins.then_inc(tm_free, 1)
                hi(act, 1, P_V + 1 + b, m, i)

            with act.Fori(0, 8) as i:
                v_block(0, 1, i)
            act.wait_ge(bna, TT)
            act.activation(rt[:, 0:TT], mv[:, :, 1], ACT.Sqrt, bias=eps[:, :]).then_inc(ln_sq, 1)

            def u_tile(n, i=None):
                s = n % 2
                act.wait_ge(ln, at(3 * n + 3, 6, i))
                if n:
                    act.wait_ge(mixed, at(n, 2, i))
                else:
                    act.wait_ge(w_used, 2 * P_U)
                act.activation(vnh[:, :, :], v[:, bass.ds(at(n, 2, i), 1), :, :].rearrange("p o t n -> p (o t) n"),
                               ACT.Copy).then_inc(vn_hi, 1)
                act.dma_start(v_rows[0].rearrange("b t n -> (b t) n")[:, bass.ds(at(128 * n, 256, i), 128)],
                              v[64:128, bass.ds(at(n, 2, i), 1), 8, :].rearrange("p o n -> p (o n)")).then_inc(v_out[s], 16)
                act.wait_ge(w_used, at(2 * P_U + n + 1, 2, i))
                if n:
                    act.wait_ge(gated, at(n, 2, i))
                for dst, src in zip(cut(u), chunks(0)):
                    ins = act.activation(dst, src, ACT.Gelu_apprx_tanh)
                ins.then_inc(free[0], 1)
                hi(act, s, P_U + 1 + n // 2, 1, i)

            u_tile(0)
            u_tile(1)
            with act.Fori(0, 7) as i:
                u_tile(2, i)
                u_tile(3, i)

            for c in range(16):
                if c == 0:
                    act.wait_ge(w_used, 2 * P_OUT)
                act.wait_ge(gated, c + 1)
                act.activation(gh[:, c, :], gt[:, c, :], ACT.Copy).then_inc(g_hi, 1)

            def squares(n, m, i=None):
                for h in range(2):
                    c = 16 * n + 2 * m + h
                    if c:
                        act.wait_ge(x_ss, at(c if n == 0 or m == 0 else c - 1, 4, i))
                    if i is not None:
                        act.sem_inc(hold_act, 1)
                    act.activation(square_slot(n, h), x_tile(m, i)[:, h * (T // 2):(h + 1) * (T // 2)], ACT.Square).then_inc(x_sq, 1)

            def out_tile(m, i=None):
                area = m % 2
                hi(act, 0, P_OUT + m + 1, 2, i)
                if m == 7:
                    return
                act.wait_ge(w_used, at(2 * (P_OUT + m) + 2, 4, i))
                if i is not None:
                    act.sem_inc(hold_act, 1)
                for dst, src in zip(cut(x_tile(m, i)), chunks(area)):
                    ins = act.activation(dst, src, ACT.Copy)
                ins.then_inc(free[area], 1)
                hi(act, 1, P_OUT + m + 1, 2, i)
                act.wait_ge(free[area], at((A_O, B_O)[area] + m // 2 + 1, 1, i))
                squares(0, m, i)

            by_pairs(act, out_tile)

            def split_hi(k, col):
                act.activation(hh[:, k, :], x[:, k, :], ACT.Identity, scale=gains[:, col + k:col + k + 1]).then_inc(h_hi, 1)

            def ffn(L):
                P, J = P_F[L], FT * L
                act.wait_ge(w_used, 2 * P)
                for k in range(KT):
                    split_hi(k, 16 + 8 * L)
                    if k == 1:
                        if L == 0:
                            for dst, src in zip(cut(x[:, 7, :]), chunks(1)):
                                ins = act.activation(dst, src, ACT.Copy)
                            ins.then_inc(free[1], 1)
                        hi(act, 1, P)
                        act.wait_ge(free[1], B_F[L])
                    if k == 3:
                        squares(2 * L, 7)
                act.wait_ge(stat, STATS[2 * L])
                for dst, src in zip(cut(rbc), chunks(1)):
                    ins = act.activation(dst, src, ACT.Sqrt, scale=1.0 / D, bias=eps[:, :])
                ins.then_inc(rb_sq, 1)

                def conv_start(q, c, i=None):
                    j = J + 2 * c + q
                    for z, dst in ((0, cg), (1, cv)):
                        act.wait_ge(halo, at(2 * j + z + 1, 4, i))
                        if z == 1 and (i is not None or j):
                            act.wait_ge(mtok, at(j, 2, i))
                        if i is not None:
                            act.sem_inc(hold_act, 1)
                        k = bass.ds(at(FT * z + 2 * c + q, 2, i), 1)
                        act.activation(dst[:, 0:CW], a_sb[:, z, 2:2 + CW], ACT.Identity, scale=cw[:, L, 1, 0, k],
                                       bias=cw[:, L, 1, 1, k]).then_inc(conv0, 1)

                def silu_hi(q, c, m=0, i=None):
                    j = J + 2 * c + q
                    act.wait_ge(conv, at(4 * j + 2, 8, i))
                    if i is not None or j:
                        act.wait_ge(mtok, at(j, 2, i))
                    act.activation(sg[:, 0:CW], cg[:, 0:CW], ACT.Silu).then_inc(silu, 1)

                def act_hi(q, c, i=None, dst=None):
                    j = J + 2 * c + q
                    act.wait_ge(mtok, at(j + 1, 2, i))
                    act.activation(fh[:, q, :] if dst is None else dst, mt[:, :], ACT.Copy).then_inc(f_hi, 1)

                def state(c, i=None):
                    n = FI * L + c
                    act.wait_ge(state_t, at(n + 1, 1, i))
                    act.activation(sto[:, :, :].rearrange("p z n -> p (z n)"), ps[0:18, 7, :], ACT.Copy).then_inc(state_o, 1)
                    act.wait_ge(state_o, at(n + 1, 1, i))
                    col = bass.ds(at(256 * c, 256, i), 256)
                    st = sto[:, :, :].rearrange("p (z q) n -> p z (q n)", z=2)
                    act.dma_start(conv_prompt[L, 0].rearrange("r (z n) -> r z n", z=2)[:, :, col], st[0:2]).then_inc(state_out, 16)
                    act.dma_start(conv_sample[L].rearrange("b r (z n) -> (b r) z n", z=2)[:, :, col], st[2:18]).then_inc(state_out, 16)

                def state_stored(c, i=None):
                    act.wait_ge(state_out, at(32 * (FI * L + c + 1), 32, i))

                hi(act, 0, P + 1)
                hi(act, 1, P + 1)
                conv_start(0, 0)
                silu_hi(0, 0)
                act_hi(0, 0)
                hi(act, 0, P + 2)
                hi(act, 1, P + 2)
                conv_start(1, 0)
                silu_hi(1, 0)
                act_hi(1, 0)
                with act.Fori(0, FI - 2) as i:
                    hi(act, 0, P + 3, 3, i)
                    state(0, i)
                    hi(act, 1, P + 3, 3, i)
                    conv_start(0, 1, i)
                    silu_hi(0, 1, 3, i)
                    hi(act, 0, P + 4, 3, i)
                    hi(act, 1, P + 4, 3, i)
                    act_hi(0, 1, i)
                    hi(act, 0, P + 5, 3, i)
                    hi(act, 1, P + 5, 3, i)
                    conv_start(1, 1, i)
                    silu_hi(1, 1, 3, i)
                    act_hi(1, 1, i)
                    state_stored(0, i)
                last, c = P + 3 * FI, FI - 1
                hi(act, 0, last - 3)
                state(c - 1)
                hi(act, 1, last - 3)
                conv_start(0, c)
                silu_hi(0, c)
                act_hi(0, c, dst=fh[:, 2, :])
                hi(act, 0, last - 2)
                hi(act, 1, last - 2)
                conv_start(1, c)
                silu_hi(1, c)
                act_hi(1, c, dst=fhx[:, 0, :])
                hi(act, 0, last - 1)
                hi(act, 1, last - 1)
                state_stored(c - 1)
                state(c)
                if L == 0:
                    for m in range(8):
                        act.wait_ge(free[m % 2], (A_F, B_F)[m % 2][0] + 62 + m // 2 + 1)
                        split_hi(m, 8)
                        if m == 4:
                            hi(act, 0, last)
                        squares(1, m)
                    hi(act, 1, last)

            ffn(0)
            attention_act(act, squares)
            ffn(1)
            for m in range(8):
                act.wait_ge(y_c, m + 1)
                act.dma_start(y_prompt[0].rearrange("(t p) n -> p t n", p=128)[:, :, 128 * m:128 * m + 128],
                              yst[:, m % 2, :, :]).then_inc(y_out[m % 2], 16)
            act.wait_ge(y_c, KT + 1)
            act.dma_start(y_sample.rearrange("b t n -> (b t) n"), ysp[:, :, :].rearrange("p k n -> p (k n)")).then_inc(ys_out, 16)

        @block.vector
        def _(dve):
            dve.memset(eps[:, :], EPS).then_inc(eps_ok, 1)
            for area in range(2):
                dve.sem_inc(free[area], 1)
            for t in range(TT):
                n = 128 if t < 8 else 64
                if t % 2 == 0:
                    dve.wait_ge(rt_sq, t // 2 + 1)
                    dve.reciprocal(rt[0:n, t:min(t + 2, TT)], rt[0:n, t:min(t + 2, TT)]).then_inc(rt_rc, 1)
                    dve.wait_ge(rt_rc, t // 2 + 1)
                dve.tensor_scalar(xin[0:n, t, :], xin[0:n, t, :], rt[0:n, t:t + 1], None, mult).then_inc(xn, 1)
            dve.wait_ge(ws_in, 16)
            dve.wait_ge(t_in, 32)
            dve.tensor_tensor(wsr[:, :, :], wsr[:, :, :], tabs[:, C_CUR:C_CUR + 128].unsqueeze(1).to_broadcast([128, GROUPS, 128]),
                              mult).then_inc(ws_msk, 1)
            for s in range(2):
                lo(dve, s, P_V)

            def spatial_weights():
                dve.wait_ge(wt_hi, 1)
                dve.tensor_tensor(wtl[:, :, :].rearrange("p (a g) n -> p a (g n)", a=2), ps[:, 3:5, :],
                                  wth[:, :, :].bitcast(f32).rearrange("p (a g) n -> p a (g n)", a=2), sub).then_inc(wt_lo, 1)
                for n, (dst, bank) in enumerate(((wsh, 7), (wsl, 6))):
                    dve.wait_ge(ws8_t, n + 1)
                    dve.tensor_tensor(dst[:, :, :], ps[:, bank, :].rearrange("p (g n) -> p g n", g=GROUPS),
                                      tabs[:, C_BLK:C_BLK + 64].unsqueeze(1).to_broadcast([128, GROUPS, 64]), mult).then_inc(ws8_ok, 1)
            dve.wait_ge(vec_ok, 1)
            for k in range(KT):
                area = k % 2
                dve.wait_ge(h_hi, k + 1)
                for dst, hi_, src in zip(cut(hl[:, k, :]), cut(hh[:, k, :].bitcast(f32)), chunks(area)):
                    ins = dve.scalar_tensor_tensor(dst, src, gains[:, k:k + 1], hi_, mult, sub)
                ins.then_inc(h_lo, 1)
                if k == 0:
                    spatial_weights()

            with dve.Fori(0, 8) as i:
                lo(dve, 0, P_V + 1, 1, i)
                for t in range(TT):
                    if t % 2 == 0:
                        dve.wait_ge(tm_free, at(t // 2 + 1, 5, i))
                    dve.bn_stats(bst[:, t, bass.ds(i, 1), :].rearrange("p o n -> p (o n)"),
                                 v[:, bass.ds(at(0, 2, i), 2), t, :]).then_inc(bn, 1)
                lo(dve, 1, P_V + 1, 1, i)
            dve.wait_ge(bn, 8 * TT)
            for t in range(TT):
                dve.bn_aggr(mv[:, t, :], bst[:, t, :, :].rearrange("p b n -> p (b n)")).then_inc(bna, 1)
            dve.wait_ge(ln_sq, 1)
            dve.reciprocal(rt[:, 0:TT], rt[:, 0:TT]).then_inc(ln_rc, 1)

            def layer_norm(n, i=None):
                s = n % 2
                vt = v[:, bass.ds(at(n, 2, i), 1), :, :].rearrange("p o t n -> p (o t) n")
                for t in range(TT):
                    row = v[:, bass.ds(at(n, 2, i), 1), t, :].rearrange("p o n -> p (o n)")
                    ins = dve.tensor_scalar(row, row, mv[:, t, 0:1], rt[:, t:t + 1], sub, mult)
                ins.then_inc(ln, 1)
                dve.wait_ge(ln_in[s], at(32 * (n // 2 + 1), 32, i))
                dve.wait_ge(ln, at(3 * n + 1, 6, i))
                dve.tensor_tensor(vt, vt, lng[:, s, :].unsqueeze(1).to_broadcast([128, TT, 128]), mult).then_inc(ln, 1)
                dve.wait_ge(ln, at(3 * n + 2, 6, i))
                dve.tensor_tensor(vt, vt, lnb[:, s, :].unsqueeze(1).to_broadcast([128, TT, 128]), add).then_inc(ln, 1)

            def v_lo(n, i=None):
                vt = v[:, bass.ds(at(n, 2, i), 1), :, :].rearrange("p o t n -> p (o t) n")
                dve.wait_ge(vn_hi, at(n + 1, 2, i))
                dve.tensor_tensor(vnl[:, :, :], vt, vnh[:, :, :].bitcast(f32), sub).then_inc(vn_lo, 1)
                lo(dve, n % 2, P_U + 1 + n // 2, 1, i)

            def gating(n, i=None):
                s = n % 2
                dve.wait_ge(mixed, at(n + 1, 2, i))
                dve.wait_ge(v_out[s], at(16 * (n // 2 + 1), 16, i))
                g = bsb[:, bass.ds(at(n // 2, 1, i), 1), :].rearrange("p o n -> p (o n)")
                out = gt[:, bass.ds(at(n, 2, i), 1), :].rearrange("p o n -> p (o n)")
                b = BANK[1]
                dve.tensor_tensor(out[:, 0:768].rearrange("p (a c n) -> p a c n", a=2, n=128),
                                  ps[:, b:b + 2, 0:384].rearrange("p a (c n) -> p a c n", n=128),
                                  g.unsqueeze(1).unsqueeze(1).to_broadcast([128, 2, 3, 128]), add)
                dve.tensor_tensor(out[:, 768:1024].rearrange("p (c n) -> p c n", n=128),
                                  ps[:, b + 2, 0:256].rearrange("p (c n) -> p c n", n=128),
                                  g.unsqueeze(1).to_broadcast([128, 2, 128]), add)
                dve.tensor_tensor(out[:, 1024:T].rearrange("p (c n) -> p c n", n=NT),
                                  ps[:, b + 2, 256:320].rearrange("p (c n) -> p c n", n=NT),
                                  g[:, 0:NT].unsqueeze(1).to_broadcast([128, NB, NT]), add).then_inc(free[1], 1)
                dve.wait_ge(free[1], at(B_U + n + 1, 2, i))
                dve.wait_ge(free[0], at(A_U + n + 1, 2, i))
                dve.tensor_tensor(out, out, u[:, :], mult).then_inc(gated, 1)

            dve.wait_ge(ln_rc, 1)
            dve.wait_ge(bs_in, 16)
            layer_norm(0)
            with dve.Fori(0, 7) as i:
                for n in range(2):
                    v_lo(n, i)
                    layer_norm(n + 1, i)
                    gating(n, i)
            v_lo(14)
            layer_norm(15)
            gating(14)
            v_lo(15)
            gating(15)

            for c in range(16):
                dve.wait_ge(g_hi, c + 1)
                dve.tensor_tensor(gl[:, c, :], gt[:, c, :], gh[:, c, :].bitcast(f32), sub).then_inc(g_lo, 1)
            with dve.Fori(0, 7) as i:
                for s in range(2):
                    lo(dve, s, P_OUT + 1, 1, i)
            lo(dve, 0, P_F[0])

            def take_y(m):
                dve.wait_ge(y_t, m + 1)
                if m >= 2:
                    dve.wait_ge(y_out[m % 2], 16 * (m // 2))
                dve.tensor_copy(yst[:, m % 2, :, :].rearrange("p (a t) n -> p a (t n)", a=2), ps[:, 6:8, :]).then_inc(y_c, 1)

            def split_lo(n, col, k):
                dve.wait_ge(h_hi, 8 * n + k + 1)
                dve.scalar_tensor_tensor(hl[:, k, :], x[:, k, :], gains[:, col + k:col + k + 1],
                                         hh[:, k, :].bitcast(f32), mult, sub).then_inc(h_lo, 1)

            def ffn(L):
                P, J = P_F[L], FT * L
                FA, FB = A_F[L], B_F[L]
                for k in range(KT):
                    split_lo(1 if L == 0 else 4, 16 + 8 * L, k)
                    if k == 1:
                        if L == 1:
                            for dst, src in zip(cut(x[:, 7, :]), chunks(1)):
                                ins = dve.tensor_tensor(dst, dst, src, add)
                            ins.then_inc(free[1], 1)
                        lo(dve, 1, P)
                lo(dve, 0, P + 1)
                dve.wait_ge(rb_sq, L + 1)
                dve.reciprocal(rbc[:, :], rbc[:, :]).then_inc(rb_ok, 1)
                dve.wait_ge(rb_ok, L + 1)
                dve.wait_ge(zero, L + 1)

                def take(z, q, area, n_area, unit, mu, c, i=None):
                    j = J + 2 * c + q
                    dve.wait_ge(w_used, at(unit + 1, mu, i))
                    b = BANK[area]
                    dve.tensor_tensor(a_sb[:, z, 2:770].rearrange("p (c n) -> p c n", c=2), ps[:, b:b + 2, 0:384],
                                      rbc[:, 0:768].rearrange("p (c n) -> p c n", c=2), mult)
                    dve.tensor_tensor(a_sb[:, z, 770:1026], ps[:, b + 2, 0:256], rbc[:, 768:1024], mult)
                    smp = a_sb[:, z, 1026:1026 + NB * STEP].rearrange("p (b n) -> p b n", n=STEP)
                    dve.tensor_tensor(smp[:, :, 2:STEP], ps[:, b + 2, 256:320].rearrange("p (b n) -> p b n", n=NT),
                                      rbc[:, 1024:T].rearrange("p (b n) -> p b n", n=NT), mult).then_inc(free[area], 1)
                    dve.wait_ge(past_t, at(FI * L + c + 1, 1, i))
                    col = (2 * z + q) * 16
                    dve.tensor_copy(smp[:, :, 0:2], ps[:, 6, col:col + 16].rearrange("p (b r) -> p b r", r=2)).then_inc(halo, 1)
                    if i is not None or J + c:
                        dve.wait_ge(state_t, at(FI * L + c, 1, i))
                    dve.wait_ge(free[area], at(n_area + 1, 6, i))
                    last = a_sb[:, z, 1024:1024 + 9 * STEP].rearrange("p (g n) -> p g n", n=STEP)[:, :, 0:2]
                    dve.tensor_copy(stc[:, 2 * z + q, :].rearrange("p (g n) -> p g n", n=2), last).then_inc(state_c, 1)
                    dve.wait_ge(halo, at(2 * j + z + 1, 4, i))

                def conv_tap(q, c, z, r, i=None):
                    j = J + 2 * c + q
                    dst = (cg, cv)[z]
                    if r == 1:
                        dve.wait_ge(conv0, at(2 * j + z + 1, 4, i))
                    else:
                        dve.wait_ge(conv, at(4 * j + 2 * z + 1, 8, i))
                    dve.scalar_tensor_tensor(dst[:, 0:CW], a_sb[:, z, r:r + CW], cw[:, L, 0, r, bass.ds(at(FT * z + 2 * c + q, 2, i), 1)],
                                             dst[:, 0:CW], mult, add).then_inc(conv, 1)

                def gate_value(q, c, i=None):
                    j = J + 2 * c + q
                    dve.wait_ge(conv, at(4 * j + 4, 8, i))
                    dve.wait_ge(silu, at(j + 1, 2, i))
                    if i is not None or j:
                        dve.wait_ge(f_lo, at(j, 2, i))
                    dve.tensor_tensor(mt[:, 0:SEQ], sg[:, 0:SEQ], cv[:, 0:SEQ], mult)
                    dve.tensor_tensor(mt[:, SEQ:T].rearrange("p (b n) -> p b n", n=NT),
                                      sg[:, SEQ + 2:SEQ + 2 + NB * STEP].rearrange("p (b n) -> p b n", n=STEP)[:, :, 0:NT],
                                      cv[:, SEQ + 2:SEQ + 2 + NB * STEP].rearrange("p (b n) -> p b n", n=STEP)[:, :, 0:NT],
                                      mult).then_inc(mtok, 1)

                def convolve(q, c, i=None):
                    for z, r in ((0, 1), (0, 0), (1, 1), (1, 0)):
                        conv_tap(q, c, z, r, i)
                    gate_value(q, c, i)

                def act_lo(q, c, i=None, dst=None, high=None):
                    j = J + 2 * c + q
                    dve.wait_ge(f_hi, at(j + 1, 2, i))
                    dve.tensor_tensor(fl[:, q, :] if dst is None else dst, mt[:, :],
                                      (fh[:, q, :] if high is None else high).bitcast(f32), sub).then_inc(f_lo, 1)

                def add_down(m, n_down, unit, n_area, i=None):
                    area = m % 2
                    if m in (3, 7):
                        dve.wait_ge(w_used, at(unit + m // 4 + 1, 6, i))
                    else:
                        dve.wait_ge(down, at(n_down + (m if m < 3 else m - 1) + 1, 6, i))
                    for dst, src in zip(cut(x[:, m, :]), chunks(area)):
                        ins = dve.tensor_tensor(dst, dst, src, add)
                    ins.then_inc(free[area], 1)

                take(0, 0, 0, FA, 2 * P, 6, 0)
                take(1, 0, 1, FB, 2 * P + 1, 6, 0)
                lo(dve, 1, P + 1)
                convolve(0, 0)
                act_lo(0, 0)
                take(0, 1, 0, FA + 1, 2 * P + 2, 6, 0)
                lo(dve, 0, P + 2)
                take(1, 1, 1, FB + 1, 2 * P + 3, 6, 0)
                lo(dve, 1, P + 2)
                convolve(1, 0)
                act_lo(1, 0)
                U = 2 * (P + 2)
                DN = 66 * L
                with dve.Fori(0, FI - 2) as i:
                    take(0, 0, 0, FA + 2, U, 6, 1, i)
                    lo(dve, 0, P + 3, 3, i)
                    take(1, 0, 1, FB + 2, U + 1, 6, 1, i)
                    lo(dve, 1, P + 3, 3, i)
                    add_down(0, DN, U + 2, None, i)
                    conv_tap(0, 1, 0, 1, i)
                    add_down(1, DN, U + 2, None, i)
                    conv_tap(0, 1, 0, 0, i)
                    add_down(2, DN, U + 2, None, i)
                    conv_tap(0, 1, 1, 1, i)
                    add_down(3, DN, U + 2, None, i)
                    lo(dve, 0, P + 4, 3, i)
                    add_down(4, DN, U + 2, None, i)
                    conv_tap(0, 1, 1, 0, i)
                    add_down(5, DN, U + 2, None, i)
                    gate_value(0, 1, i)
                    add_down(6, DN, U + 2, None, i)
                    add_down(7, DN, U + 2, None, i)
                    lo(dve, 1, P + 4, 3, i)
                    act_lo(0, 1, i)
                    take(0, 1, 0, FA + 7, U + 4, 6, 1, i)
                    lo(dve, 0, P + 5, 3, i)
                    take(1, 1, 1, FB + 7, U + 5, 6, 1, i)
                    lo(dve, 1, P + 5, 3, i)
                    convolve(1, 1, i)
                    act_lo(1, 1, i)
                last, c, r = P + 3 * FI, FI - 1, 6 * (FI - 2)
                take(0, 0, 0, FA + 2 + r, 2 * (last - 4), 6, c)
                lo(dve, 0, last - 3)
                take(1, 0, 1, FB + 2 + r, 2 * (last - 4) + 1, 6, c)
                lo(dve, 1, last - 3)
                convolve(0, c)
                act_lo(0, c, dst=fl[:, 2, :], high=fh[:, 2, :])
                take(0, 1, 0, FA + 3 + r, 2 * (last - 3), 6, c)
                lo(dve, 0, last - 2)
                take(1, 1, 1, FB + 3 + r, 2 * (last - 3) + 1, 6, c)
                lo(dve, 1, last - 2)
                for m in range(8):
                    add_down(m, DN + r, 2 * (last - 2), None)
                    if m in (0, 1):
                        conv_tap(1, c, 0, 1 - m)
                    if m in (2, 4):
                        conv_tap(1, c, 1, (4 - m) // 2)
                    if m == 5:
                        gate_value(1, c)
                    if m == 6:
                        act_lo(1, c, dst=flx[:, 0, :], high=fhx[:, 0, :])
                lo(dve, 0, last - 1)
                lo(dve, 1, last - 1)
                for m in range(8):
                    if L == 1 and m >= 2:
                        take_y(m - 2)
                    add_down(m, DN + 6 * (FI - 1), 2 * (last - 1), None)
                    if L == 0 and m:
                        split_lo(2, 8, m - 1)
                    if L == 0 and m == 6:
                        lo(dve, 0, last)
                if L == 0:
                    split_lo(2, 8, 7)
                    lo(dve, 1, last)

            ffn(0)
            attention_dve(dve)
            ffn(1)
            for m in (6, 7):
                take_y(m)
            dve.wait_ge(y_t, KT + 1)
            dve.tensor_copy(ysp[:, :, :].rearrange("p (a k) n -> p a (k n)", a=2), ps[0:64, 0:2, :]).then_inc(y_c, 1)

        @block.tensor
        def _(pe):
            pe.wait_ge(t_in, 32)
            pe.wait_ge(vec_in, 160)
            pe.transpose(ps[:, 6, 0:32], vecs[0:32, 0, :], idn[0:32, 0:32])
            for n in range(4):
                ins = pe.transpose(ps[:, 6, 32 + 88 * n:120 + 88 * n], vecs[0:88, 1 + n, :], idn[0:88, 0:88])
            ins.then_inc(vec_t, 1)

            def transpose_x(k):
                for t in range(TT):
                    n = 128 if t < 8 else 64
                    ins = pe.transpose(ps[:, BANK[k % 2] + t // 3, (t % 3) * 128:(t % 3) * 128 + n],
                                       xin[0:n, t, 128 * k:128 * k + 128], idn[0:n, 0:n])
                ins.then_inc(x_t, 1)

            pe.wait_ge(xn, TT)
            transpose_x(0)
            pe.wait_ge(ws_msk, 1)
            for g in range(GROUPS):
                ins = pe.transpose(ps[:, 3 + g // 4, (g % 4) * 128:(g % 4) * 128 + 128], wsr[:, g, :], idn[:, :])
            ins.then_inc(ws_t, 1)
            pe.wait_ge(sel_ok, 1)
            pe.wait_ge(wt_hi, 1)
            pe.wait_ge(vec_ok, 2)
            for src, bank, done in ((wth, 7, None), (wtl, 6, wt_lo)):
                if done is not None:
                    pe.wait_ge(done, 1)
                for g in range(GROUPS):
                    ins = pe.matmul(ps[:, bank, 64 * g:64 * g + 64], selr[:, :],
                                    src[:, g, 0:NT].unsqueeze(1).to_broadcast([128, NB, NT]), start=True, stop=True)
                ins.then_inc(ws8_t, 1)
            for k in range(1, KT):
                if k >= 2:
                    pe.wait_ge(h_lo, k - 1)
                transpose_x(k)

            def token_major(p0, n0, m=0, i=None, first=None):
                for s in range(2):
                    pe.wait_ge(w_lo, at(2 * p0 + s + 1, 2 * m, i))
                    order = [(k, t) for k in range(4) for t in range(TT)] if s == 0 else \
                            [(k, t) for t in range(TT) for k in range(4)]
                    for k, t in order:
                        if first is not None and s == 0 and t == 0:
                            pe.wait_ge(h_lo, first + (k + 1 if k < 3 else KT))
                        if s == 0 and k == 0 and t % 2 == 0 and n0 is not None:
                            pe.wait_ge(tm_free, at(5 * n0 + t // 2 + 1, 5 * m, i))
                        o = ps[:, t // 2, (t % 2) * 256:(t % 2) * 256 + 256]
                        for n, (a, w) in enumerate(((hh, wh), (hh, wl), (hl, wh))):
                            ins = pe.matmul(o, a[:, 4 * s + k, TOK0[t]:TOK0[t] + 128], w[:, s, 256 * k:256 * k + 256],
                                            start=s == 0 and k == 0 and n == 0 and t % 2 == 0,
                                            stop=s == 1 and k == 3 and n == 2, skip_group_check=True)
                        if s == 1 and k == 3 and t < 8 and t % 2:
                            ins.then_inc(tm_full, 1)
                    ins.then_inc(w_used, 1)

            pe.wait_ge(h_lo, KT)
            pe.wait_ge(ws8_ok, 2)
            token_major(P_V, None)
            with pe.Fori(0, 7) as i:
                token_major(P_V + 1, 0, 1, i)

            pe.wait_ge(tm_free, 40)
            with pe.Fori(0, 8) as i:
                for s in range(2):
                    if s:
                        pe.wait_ge(free[0], at(A_U + 1, 2, i))
                    else:
                        pe.wait_ge(free[0], at(A_U, 2, i))
                    pe.wait_ge(w_lo, at(2 * P_U + s + 1, 2, i))
                    for k in range(KT):
                        ins = rows(pe, 0, s, k, 128 * k, x_mov, k == 0, k == 7)
                    ins.then_inc(w_used, 1)
                    pe.wait_ge(vn_lo, at(s + 1, 2, i))
                    pe.wait_ge(free[1], at(B_U + s, 2, i))
                    for t in range(TT):
                        n = 128 if t < 8 else 64
                        gi = bass.ds(i, 1)
                        src = (wth, wtl) if t < 8 else (wsh, wsl)
                        o = ps[:, 3 + t // 3, (t % 3) * 128:(t % 3) * 128 + n]
                        for r, (a, w) in enumerate(((vnh, src[0]), (vnh, src[1]), (vnl, src[0]))):
                            ins = pe.matmul(o, a[:, t, :], w[:, gi, :].rearrange("p o n -> p (o n)"),
                                            start=r == 0, stop=r == 2)
                    ins.then_inc(mixed, 1)

            def out_tile(m, i=None):
                area = m % 2
                pe.wait_ge(free[area], at((A_O, B_O)[area] + m // 2, 1, i))
                for s in range(2):
                    pe.wait_ge(w_lo, at(2 * (P_OUT + m) + s + 1, 4, i))
                    for k in range(8):
                        if m == 0:
                            pe.wait_ge(g_lo, 8 * s + k + 1)
                        ins = rows(pe, area, s, 8 * s + k, 128 * k, g_mov, s == 0 and k == 0, s == 1 and k == 7)
                    ins.then_inc(w_used, 1)
                    if s == 0:
                        pe.wait_ge(xm_in, at(32 * (m + 1), 64, i))
                        for t in range(TT):
                            n = 128 if t < 8 else 64
                            ins = pe.matmul(ps[:, BANK[area] + t // 3, (t % 3) * 128:(t % 3) * 128 + n], xm[0:n, t, :],
                                            idn[0:n, 0:n], start=False, stop=False, skip_group_check=True)
                        ins.then_inc(xm_used, 1)

            by_pairs(pe, out_tile)

            def transpose_y(m):
                if m == 0:
                    pe.wait_ge(state_o, 2 * FI)
                    pe.wait_ge(halo, 4 * 2 * FI)
                else:
                    pe.wait_ge(y_c, m)
                for t in range(8):
                    ins = pe.transpose(ps[:, 6 + t // 4, (t % 4) * 128:(t % 4) * 128 + 128], x[:, m, 128 * t:128 * t + 128], idn[:, :])
                ins.then_inc(y_t, 1)

            def ffn(L):
                P, J = P_F[L], FT * L
                FA, FB = A_F[L], B_F[L]

                def past(c, i=None):
                    n = FI * L + c
                    pe.wait_ge(past_in, at(16 * (n + 1), 16, i))
                    if i is not None or n:
                        pe.wait_ge(halo, at(4 * n, 4, i))
                    for z in range(4):
                        ins = pe.matmul(ps[:, 6, 16 * z:16 * z + 16], pst[:, z, :], idn[0:16, 0:16], start=True, stop=True)
                    ins.then_inc(past_t, 1)

                def state(c, i=None):
                    n = FI * L + c
                    pe.wait_ge(state_c, at(4 * (n + 1), 4, i))
                    for z in range(4):
                        ins = pe.transpose(ps[0:18, 7, 128 * z:128 * z + 128], stc[:, z, :], idn[:, :])
                    ins.then_inc(state_t, 1)

                def up(s, area, n_area, p, m=0, i=None, inside=None, first=False):
                    pe.wait_ge(free[area], at(n_area, 6, i))
                    pe.wait_ge(w_lo, at(2 * p + s + 1, 2 * m, i))
                    for k in range(KT):
                        if first:
                            pe.wait_ge(h_lo, 8 * (1 if L == 0 else 4) + k + 1)
                        if k == 6 and inside is not None:
                            inside()
                        ins = rows(pe, area, s, k, 128 * k, x_mov, k == 0, k == 7)
                    ins.then_inc(w_used, 1)

                def down_proj(na, nb, p, m_=0, i=None, last=False):
                    for m in range(8):
                        area, s = m % 2, m // 4
                        pe.wait_ge(free[area], at((na, nb)[area] + m // 2, 6, i))
                        if last and L == 1 and m >= 2:
                            transpose_y(m - 2)
                        if m % 4 == 0:
                            pe.wait_ge(w_lo, at(2 * p + s + 1, 2 * m_, i))
                        for k in range(2):
                            mov, slot = (((fh, fl), 2), ((fhx, flx), 0))[k] if last else ((fh, fl), k)
                            ins = rows(pe, area, s, slot, 512 * k + 128 * (m % 4), mov, k == 0, k == 1)
                        ins.then_inc(w_used if m % 4 == 3 else down, 1)

                up(0, 0, FA, P, inside=lambda: past(0), first=True)
                pe.wait_ge(x_ss, 16 * (L + 1 + (L == 1)))
                pe.wait_ge(free[1], FB)
                pe.wait_ge(ones_ok, 1)
                for c, (c0, cn) in enumerate(CH):
                    ins = pe.matmul(ps[:, 3 + c, 0:cn], ones[:, :], ssum[:, c0:c0 + cn], start=True, stop=True)
                ins.then_inc(stat, 1)
                pe.wait_ge(rb_sq, L + 1)
                up(1, 1, FB, P)
                up(0, 0, FA + 1, P + 1)
                up(1, 1, FB + 1, P + 1)
                with pe.Fori(0, FI - 2) as i:
                    def edge():
                        past(1, i)
                        state(0, i)
                    up(0, 0, FA + 2, P + 2, 3, i, inside=edge)
                    up(1, 1, FB + 2, P + 2, 3, i)
                    pe.wait_ge(f_lo, at(J + 2, 2, i))
                    down_proj(FA + 3, FB + 3, P + 3, 3, i)
                    up(0, 0, FA + 7, P + 4, 3, i)
                    up(1, 1, FB + 7, P + 4, 3, i)
                    pe.wait_ge(state_o, at(FI * L + 1, 1, i))
                c, r, last = FI - 1, 6 * (FI - 2), P + 3 * FI

                def last_edge():
                    past(c)
                    state(c - 1)
                up(0, 0, FA + 2 + r, last - 4, inside=last_edge)
                up(1, 1, FB + 2 + r, last - 4)
                up(0, 0, FA + 3 + r, last - 3)
                up(1, 1, FB + 3 + r, last - 3)
                pe.wait_ge(f_lo, J + 2 * c)
                down_proj(FA + 4 + r, FB + 4 + r, last - 2)
                pe.wait_ge(state_o, FI * L + c)
                state(c)
                pe.wait_ge(f_lo, J + 2 * FI)
                down_proj(FA + 8 + r, FB + 8 + r, last - 1, last=True)

            ffn(0)
            attention_pe(pe, token_major)
            attention_out_pe(pe)
            ffn(1)
            for m in (6, 7):
                pe.wait_ge(free[m % 2], (A_END, B_END)[m % 2])
                transpose_y(m)
            for m in range(KT):
                ins = pe.transpose(ps[0:64, m // 4, (m % 4) * 128:(m % 4) * 128 + 128], x[:, m, SEQ:T], idn[:, :])
            ins.then_inc(y_t, 1)


_INS = ['x_prompt', 'x_sample', 'cache_swa_k', 'cache_swa_v', 'state_ffn_conv', 'mix_norm_g', 'sgu_w_in', 'sgu_ln_g',
        'sgu_ln_b', 'sgu_w_s', 'sgu_b_s', 'sgu_w_out', 'attn_w_qkv', 'attn_q_norm', 'attn_k_norm', 'attn_sinks',
        'attn_w_o', 'ffn_norm_g', 'ffn_w_up', 'ffn_conv_w', 'ffn_conv_b', 'ffn_w_down']
_OUTS = [(1, SEQ, D), (NB, NT, D), (1, NB, NT, SGU), (1, 1, 128, NKV, HD), (1, 1, 128, NKV, HD),
         (1, NB, 128, NKV, HD), (1, NB, 128, NKV, HD), (2, 1, 2, 2 * DFF), (2, NB, 2, 2 * DFF)]


def kernel(**inputs):
    import concourse.bacc as _bacc
    from concourse.bass_utils import run_bass_kernel_spmd as _run

    nc = _bacc.Bacc("TRN2", target_bir_lowering=False, num_devices=1)
    arrays, args = {}, []
    table, rotary = constants()
    for name, a in [(n, inputs[n]) for n in _INS] + [("table", table), ("rotary", rotary)]:
        a = np.ascontiguousarray(a)
        arrays[f"in_{name}"] = a
        args.append(nc.dram_tensor(f"in_{name}", a.shape, mybir.dt.from_np(a.dtype), kind="ExternalInput").ap())
    for i, shape in enumerate(_OUTS):
        args.append(nc.dram_tensor(f"out_{i}", shape, mybir.dt.float32, kind="ExternalOutput").ap())
    step_program(nc, *args)
    r = _run(nc, [arrays], core_ids=[0])
    return tuple(r.results[0][f"out_{i}"] for i in range(len(_OUTS)))
```
